# Optimizing a Trainium2 kernel written in Bass

```python
import math
import jax
import jax.numpy as jnp
from jax import lax
import numpy as np
import jax, jax.numpy as jnp

D_MODEL = 1024
BATCH = 1
SEQ = 1024
DEPTH = 1

CHUNK = 64
Q_BLOCK = 128
GMLP_BLOCK = 128

A_GROUPS = 4
A_GDIM = 64
A_WIDTH = A_GROUPS * A_GDIM
B_HEADS = 4
B_QK_DIM = 64
B_V_DIM = 2 * B_QK_DIM
B_WIDTH = B_HEADS * B_V_DIM
C_HEADS = 4
C_HEAD_DIM = 64
C_WIDTH = C_HEADS * C_HEAD_DIM
IDX_HEADS = 8
IDX_DIM = 32
TOPK_MAX = 256
MIX_WIDTH = A_WIDTH + B_WIDTH + C_WIDTH

FFN_HIDDEN = -(-8 * D_MODEL // (3 * 256)) * 256

OFF_A_U = 0
OFF_A_V = OFF_A_U + A_WIDTH
OFF_B_Q = OFF_A_V + A_WIDTH
OFF_B_K = OFF_B_Q + B_HEADS * 2 * B_QK_DIM
OFF_B_V = OFF_B_K + B_HEADS * 2 * B_QK_DIM
OFF_C_Q = OFF_B_V + B_WIDTH
OFF_C_K = OFF_C_Q + C_WIDTH
OFF_C_V = OFF_C_K + C_WIDTH
OFF_I_Q = OFF_C_V + C_WIDTH
OFF_I_K = OFF_I_Q + IDX_HEADS * IDX_DIM
OFF_I_W = OFF_I_K + IDX_DIM
IN_WIDTH = OFF_I_W + IDX_HEADS

DEEPNORM_ALPHA = (2 * DEPTH) ** 0.25
DEEPNORM_BETA = (8 * DEPTH) ** -0.25
LN_EPS = 1e-5


def layer_norm(x, g, b):
    xf = x.astype(jnp.float32)
    mu = jnp.mean(xf, axis=-1, keepdims=True)
    xc = xf - mu
    var = jnp.mean(xc * xc, axis=-1, keepdims=True)
    return (xc * lax.rsqrt(var + LN_EPS) * g.astype(jnp.float32) + b.astype(jnp.float32)).astype(x.dtype)

def rms_norm(x, g):
    xf = x.astype(jnp.float32)
    ms = jnp.mean(xf * xf, axis=-1, keepdims=True)
    return (xf * lax.rsqrt(ms + LN_EPS) * g.astype(jnp.float32)).astype(x.dtype)

def alibi_slopes(n):
    return jnp.asarray([2.0 ** (-8.0 * (h + 1) / n) for h in range(n)], dtype=jnp.float32)

def to_blocks(a, size):
    bn, s = a.shape[:2]
    return jnp.moveaxis(a.reshape((bn, s // size, size) + a.shape[2:]), 1, 0)

def from_blocks(a):
    n, bn, t = a.shape[:3]
    return jnp.moveaxis(a, 0, 1).reshape((bn, n * t) + a.shape[3:])

def gmlp_mixer(u, v, w_s, b_s, ln_g, ln_b):
    bn, s, _ = u.shape
    nblk = s // GMLP_BLOCK
    u = jax.nn.gelu(u)
    v = jax.nn.gelu(v).reshape(bn, nblk, GMLP_BLOCK, A_GROUPS, A_GDIM)
    v = layer_norm(v, ln_g, ln_b)
    pos_chunk = jnp.arange(GMLP_BLOCK) // CHUNK
    mask = pos_chunk[None, :] <= pos_chunk[:, None]
    w = jnp.where(mask[None], w_s, jnp.zeros_like(w_s))
    sg = jnp.einsum('gts,bnsgc->bntgc', w, v) + b_s.T[None, None, :, :, None]
    return u * sg.reshape(bn, s, A_WIDTH)

def diff_attention(q, k, v, lam, lam_init, subln_g):
    bn, s = q.shape[:2]
    nblk = s // Q_BLOCK
    scale = B_QK_DIM ** -0.5
    slopes = alibi_slopes(B_HEADS)
    kpos = jnp.arange(s)
    kchunk = kpos // CHUNK

    def block(args):
        qblk, i = args
        qpos = i * Q_BLOCK + jnp.arange(Q_BLOCK)
        allowed = kchunk[None, :] <= (qpos // CHUNK)[:, None]
        dist = jnp.abs(qpos[:, None] - kpos[None, :]).astype(jnp.float32)
        bias = -slopes[:, None, None] * dist[None]
        logits = jnp.einsum('bthmd,bshmd->bhmts', qblk, k).astype(jnp.float32) * scale
        logits = logits + bias[None, :, None]
        logits = jnp.where(allowed[None, None, None], logits, -jnp.inf)
        p = jax.nn.softmax(logits, axis=-1)
        attn = p[:, :, 0] - lam * p[:, :, 1]
        return jnp.einsum('bhts,bshe->bthe', attn.astype(v.dtype), v)

    o = from_blocks(lax.map(block, (to_blocks(q, Q_BLOCK), jnp.arange(nblk))))
    o = rms_norm(o, subln_g) * (1.0 - lam_init)
    return o.reshape(bn, s, B_WIDTH)

def dsa_attention(q, k, v, qi, ki, wi):
    bn, s = q.shape[:2]
    nblk = s // Q_BLOCK
    topk = min(TOPK_MAX, s // 4)
    scale = C_HEAD_DIM ** -0.5
    idx_scale = (IDX_HEADS ** -0.5) * (IDX_DIM ** -0.5)
    slopes = alibi_slopes(C_HEADS)
    kchunk = jnp.arange(s) // CHUNK

    def block(args):
        qblk, qiblk, wiblk, i = args
        qpos = i * Q_BLOCK + jnp.arange(Q_BLOCK)
        qchunk = qpos // CHUNK
        allowed = kchunk[None, :] <= qchunk[:, None]
        idx_logits = jnp.einsum('bthd,bsd->bths', qiblk, ki).astype(jnp.float32)
        score = jnp.einsum('bth,bths->bts', wiblk.astype(jnp.float32) * idx_scale, jax.nn.relu(idx_logits))
        score = jnp.where(allowed[None], score, -jnp.inf)
        _, sel = lax.top_k(score, topk)
        sel_ok = (sel // CHUNK) <= qchunk[None, :, None]
        k_sel = jax.vmap(lambda kb, ib: kb[ib])(k, sel)
        v_sel = jax.vmap(lambda vb, ib: vb[ib])(v, sel)
        logits = jnp.einsum('bthd,btkhd->bhtk', qblk, k_sel).astype(jnp.float32) * scale
        dist = jnp.abs(qpos[None, :, None] - sel).astype(jnp.float32)
        logits = logits - slopes[None, :, None, None] * dist[:, None]
        logits = jnp.where(sel_ok[:, None], logits, -jnp.inf)
        p = jax.nn.softmax(logits, axis=-1)
        return jnp.einsum('bhtk,btkhd->bthd', p.astype(v_sel.dtype), v_sel)

    xs = (to_blocks(q, Q_BLOCK), to_blocks(qi, Q_BLOCK), to_blocks(wi, Q_BLOCK), jnp.arange(nblk))
    o = from_blocks(lax.map(block, xs))
    return o.reshape(bn, s, C_WIDTH)

def hybrid_layer(x, layer_idx, w_in, w_s, b_s, a_ln_g, a_ln_b, lam_q1, lam_k1, lam_q2, lam_k2,
                 subln_g, w_out, ln1_g, ln1_b, w_gu, w_down, ln2_g, ln2_b):
    bn, s, _ = x.shape
    h = jnp.einsum('bsd,de->bse', x, w_in)
    a_u = h[..., OFF_A_U:OFF_A_V]
    a_v = h[..., OFF_A_V:OFF_B_Q]
    b_q = h[..., OFF_B_Q:OFF_B_K].reshape(bn, s, B_HEADS, 2, B_QK_DIM)
    b_k = h[..., OFF_B_K:OFF_B_V].reshape(bn, s, B_HEADS, 2, B_QK_DIM)
    b_v = h[..., OFF_B_V:OFF_C_Q].reshape(bn, s, B_HEADS, B_V_DIM)
    c_q = h[..., OFF_C_Q:OFF_C_K].reshape(bn, s, C_HEADS, C_HEAD_DIM)
    c_k = h[..., OFF_C_K:OFF_C_V].reshape(bn, s, C_HEADS, C_HEAD_DIM)
    c_v = h[..., OFF_C_V:OFF_I_Q].reshape(bn, s, C_HEADS, C_HEAD_DIM)
    i_q = h[..., OFF_I_Q:OFF_I_K].reshape(bn, s, IDX_HEADS, IDX_DIM)
    i_k = h[..., OFF_I_K:OFF_I_W]
    i_w = h[..., OFF_I_W:IN_WIDTH]

    out_a = gmlp_mixer(a_u, a_v, w_s, b_s, a_ln_g, a_ln_b)

    lam_init = 0.8 - 0.6 * math.exp(-0.3 * layer_idx)
    lam = (jnp.exp(jnp.sum(lam_q1.astype(jnp.float32) * lam_k1.astype(jnp.float32)))
           - jnp.exp(jnp.sum(lam_q2.astype(jnp.float32) * lam_k2.astype(jnp.float32))) + lam_init)
    out_b = diff_attention(b_q, b_k, b_v, lam, lam_init, subln_g)

    out_c = dsa_attention(c_q, c_k, c_v, i_q, i_k, i_w)

    mix = jnp.concatenate([out_a, out_b, out_c], axis=-1)
    x = layer_norm(DEEPNORM_ALPHA * x + jnp.einsum('bse,ed->bsd', mix, w_out), ln1_g, ln1_b)

    gu = jnp.einsum('bsd,df->bsf', x, w_gu)
    gate, up = gu[..., :FFN_HIDDEN], gu[..., FFN_HIDDEN:]
    ffn = jnp.einsum('bsf,fd->bsd', jax.nn.silu(gate) * up, w_down)
    return layer_norm(DEEPNORM_ALPHA * x + ffn, ln2_g, ln2_b)

def first_inputs(seed: int = 0) -> dict:
    key = jax.random.key(seed)
    ks = jax.random.split(key, 20)
    f32 = jnp.float32
    nrm = lambda k, shape: jax.random.normal(k, shape, dtype=f32)
    return {
        'x': nrm(ks[0], (BATCH, SEQ, D_MODEL)),
        'w_in': nrm(ks[1], (DEPTH, D_MODEL, IN_WIDTH)) * D_MODEL ** -0.5,
        'gmlp_w_s': nrm(ks[2], (DEPTH, A_GROUPS, GMLP_BLOCK, GMLP_BLOCK)) * GMLP_BLOCK ** -0.5,
        'gmlp_b_s': 1.0 + 0.1 * nrm(ks[3], (DEPTH, A_GROUPS, GMLP_BLOCK)),
        'gmlp_ln_g': 1.0 + 0.05 * nrm(ks[4], (DEPTH, A_GROUPS, A_GDIM)),
        'gmlp_ln_b': 0.02 * nrm(ks[5], (DEPTH, A_GROUPS, A_GDIM)),
        'lam_q1': 0.1 * nrm(ks[6], (DEPTH, B_QK_DIM)),
        'lam_k1': 0.1 * nrm(ks[7], (DEPTH, B_QK_DIM)),
        'lam_q2': 0.1 * nrm(ks[8], (DEPTH, B_QK_DIM)),
        'lam_k2': 0.1 * nrm(ks[9], (DEPTH, B_QK_DIM)),
        'diff_subln_g': 1.0 + 0.05 * nrm(ks[10], (DEPTH, B_V_DIM)),
        'w_out': nrm(ks[11], (DEPTH, MIX_WIDTH, D_MODEL)) * MIX_WIDTH ** -0.5 * DEEPNORM_BETA,
        'ln1_g': 1.0 + 0.05 * nrm(ks[12], (DEPTH, D_MODEL)),
        'ln1_b': 0.02 * nrm(ks[13], (DEPTH, D_MODEL)),
        'w_gu': nrm(ks[14], (DEPTH, D_MODEL, 2 * FFN_HIDDEN)) * D_MODEL ** -0.5,
        'w_down': nrm(ks[15], (DEPTH, FFN_HIDDEN, D_MODEL)) * FFN_HIDDEN ** -0.5 * DEEPNORM_BETA,
        'ln2_g': 1.0 + 0.05 * nrm(ks[16], (DEPTH, D_MODEL)),
        'ln2_b': 0.02 * nrm(ks[17], (DEPTH, D_MODEL)),
    }

def first_block(x, w_in, gmlp_w_s, gmlp_b_s, gmlp_ln_g, gmlp_ln_b, lam_q1, lam_k1, lam_q2, lam_k2,
              diff_subln_g, w_out, ln1_g, ln1_b, w_gu, w_down, ln2_g, ln2_b):
    for l in range(DEPTH):
        x = hybrid_layer(x, l, w_in[l], gmlp_w_s[l], gmlp_b_s[l], gmlp_ln_g[l], gmlp_ln_b[l],
                         lam_q1[l], lam_k1[l], lam_q2[l], lam_k2[l], diff_subln_g[l], w_out[l],
                         ln1_g[l], ln1_b[l], w_gu[l], w_down[l], ln2_g[l], ln2_b[l])
    return x


A_HEADS = 8
A_HEAD_DIM = D_MODEL // 16
A_WIDTH_2 = A_HEADS * A_HEAD_DIM
POOL_WINDOWS = (2, 4, 8, 16)
POOL_GROUPS = len(POOL_WINDOWS)
POOL_WIDTH = D_MODEL // 4
POOL_GROUP_DIM = POOL_WIDTH // POOL_GROUPS
CONV_WIDTH = D_MODEL // 4
CONV_K = 3
N_BRANCH = 3
MIX_WIDTH_2 = A_WIDTH_2 + POOL_WIDTH + CONV_WIDTH
D_FF = 4 * D_MODEL
RMS_EPS = 1e-6
NEG_INF = -1e30
IN_COLS = 3 * A_WIDTH_2 + A_HEADS + POOL_WIDTH + 3 * CONV_WIDTH + N_BRANCH * D_MODEL


def rmsnorm(x, g):
    xf = x.astype(jnp.float32)
    y = xf * lax.rsqrt(jnp.mean(xf * xf, axis=-1, keepdims=True) + RMS_EPS)
    return (y * g.astype(jnp.float32)).astype(x.dtype)

def forgetting_attention(q, k, v, f_logit):
    b, s, h, dh = q.shape
    q = q.transpose(0, 2, 1, 3)
    k = k.transpose(0, 2, 1, 3)
    v = v.transpose(0, 2, 1, 3)
    log_f = jax.nn.log_sigmoid(f_logit.astype(jnp.float32))
    cum_f = jnp.cumsum(log_f, axis=1).transpose(0, 2, 1)
    scale = dh ** -0.5
    outs = []
    for i in range(s // Q_BLOCK):
        qs, qe = i * Q_BLOCK, (i + 1) * Q_BLOCK
        qb = q[:, :, qs:qe]
        kb = k[:, :, :qe]
        vb = v[:, :, :qe]
        logits = jnp.einsum('bhqd,bhkd->bhqk', qb, kb).astype(jnp.float32) * scale
        logits = logits + cum_f[:, :, qs:qe, None] - cum_f[:, :, None, :qe]
        causal = jnp.arange(qs, qe)[:, None] >= jnp.arange(qe)[None, :]
        logits = jnp.where(causal[None, None], logits, NEG_INF)
        p = jax.nn.softmax(logits, axis=-1).astype(v.dtype)
        outs.append(jnp.einsum('bhqk,bhkd->bhqd', p, vb))
    o = jnp.concatenate(outs, axis=2)
    return o.transpose(0, 2, 1, 3).reshape(b, s, h * dh)

def pool_mixer(u, w_pool, pool_scale):
    b, s, _ = u.shape
    uf = u.astype(jnp.float32)
    cs = jnp.cumsum(uf, axis=1)
    groups = []
    for g, w in enumerate(POOL_WINDOWS):
        sl = slice(g * POOL_GROUP_DIM, (g + 1) * POOL_GROUP_DIM)
        cs_g = cs[..., sl]
        lagged = jnp.pad(cs_g, ((0, 0), (w, 0), (0, 0)))[:, :s]
        count = jnp.minimum(jnp.arange(1, s + 1, dtype=jnp.float32), float(w))
        groups.append((cs_g - lagged) / count[None, :, None] - uf[..., sl])
    p = jnp.stack(groups, axis=2).astype(u.dtype)
    y = jnp.einsum('bsgc,gcd->bsgd', p, w_pool).reshape(b, s, POOL_WIDTH)
    return y * pool_scale

def short_conv(h, b_gate, c_gate, conv_w):
    u = c_gate * h
    y = lax.conv_general_dilated(
        u, conv_w[:, None, :].astype(u.dtype), window_strides=(1,), padding=[(CONV_K - 1, 0)],
        dimension_numbers=('NWC', 'WIO', 'NWC'), feature_group_count=CONV_WIDTH)
    return b_gate * y

def hybrid_layer_2(x, c, w_ada, b_ada, g_mix_pre, g_mix_post, g_ff_pre, g_ff_post, w_in, b_f,
                 w_pool, pool_scale, conv_w, w_branch, w_out, w_ff1, w_ff2):
    b, s, d = x.shape
    mod = jax.nn.silu(c) @ w_ada + b_ada
    shift_m, scale_m, gate_m, shift_f, scale_f, gate_f = jnp.split(mod, 6, axis=-1)

    h = rmsnorm(x, g_mix_pre) * (1.0 + scale_m[:, None]) + shift_m[:, None]
    z = h @ w_in
    sizes = [A_WIDTH_2, A_WIDTH_2, A_WIDTH_2, A_HEADS, POOL_WIDTH, CONV_WIDTH, CONV_WIDTH, CONV_WIDTH]
    cuts = [int(v) for v in np.cumsum(sizes)]
    q, k, v, fl, pu, ch, cb, cc, gl = jnp.split(z, cuts, axis=-1)
    heads = (b, s, A_HEADS, A_HEAD_DIM)
    br_a = forgetting_attention(q.reshape(heads), k.reshape(heads), v.reshape(heads), fl + b_f)
    br_b = pool_mixer(pu, w_pool, pool_scale)
    br_c = short_conv(ch, cb, cc, conv_w)
    gates = jax.nn.sigmoid(gl).reshape(b, s, N_BRANCH, d)
    wa = w_branch[:A_WIDTH_2]
    wb = w_branch[A_WIDTH_2:A_WIDTH_2 + POOL_WIDTH]
    wc = w_branch[A_WIDTH_2 + POOL_WIDTH:]
    merged = gates[:, :, 0] * (br_a @ wa) + gates[:, :, 1] * (br_b @ wb) + gates[:, :, 2] * (br_c @ wc)
    y = merged @ w_out
    x = x + gate_m[:, None] * rmsnorm(y, g_mix_post)

    h2 = rmsnorm(x, g_ff_pre) * (1.0 + scale_f[:, None]) + shift_f[:, None]
    y2 = jnp.square(jax.nn.relu(h2 @ w_ff1)) @ w_ff2
    return x + gate_f[:, None] * rmsnorm(y2, g_ff_post)

def second_inputs(seed: int = 0) -> dict:
    key = jax.random.key(seed)
    ks = jax.random.split(key, 20)

    def nrm(k, shape, std):
        return jax.random.normal(k, shape, jnp.float32) * std

    d = D_MODEL
    branch_row_scale = jnp.concatenate([
        jnp.full((A_WIDTH_2,), A_WIDTH_2 ** -0.5, jnp.float32),
        jnp.full((POOL_WIDTH,), POOL_WIDTH ** -0.5, jnp.float32),
        jnp.full((CONV_WIDTH,), CONV_WIDTH ** -0.5, jnp.float32)])
    return {
        'x': nrm(ks[0], (BATCH, SEQ, d), 1.0),
        'c': nrm(ks[1], (BATCH, d), 1.0),
        'w_ada': nrm(ks[2], (DEPTH, d, 6 * d), 0.5 * d ** -0.5),
        'b_ada': nrm(ks[3], (DEPTH, 6 * d), 0.02),
        'g_mix_pre': 1.0 + nrm(ks[4], (DEPTH, d), 0.05),
        'g_mix_post': 1.0 + nrm(ks[5], (DEPTH, d), 0.05),
        'g_ff_pre': 1.0 + nrm(ks[6], (DEPTH, d), 0.05),
        'g_ff_post': 1.0 + nrm(ks[7], (DEPTH, d), 0.05),
        'w_in': nrm(ks[8], (DEPTH, d, IN_COLS), d ** -0.5),
        'b_f': 3.0 + nrm(ks[9], (DEPTH, A_HEADS), 0.1),
        'w_pool': nrm(ks[10], (DEPTH, POOL_GROUPS, POOL_GROUP_DIM, POOL_GROUP_DIM), POOL_GROUP_DIM ** -0.5),
        'pool_scale': 1.0 + nrm(ks[11], (DEPTH, POOL_WIDTH), 0.1),
        'conv_w': nrm(ks[12], (DEPTH, CONV_K, CONV_WIDTH), CONV_K ** -0.5),
        'w_branch': nrm(ks[13], (DEPTH, MIX_WIDTH_2, d), 1.0) * branch_row_scale[None, :, None],
        'w_out': nrm(ks[14], (DEPTH, d, d), d ** -0.5),
        'w_ff1': nrm(ks[15], (DEPTH, d, D_FF), d ** -0.5),
        'w_ff2': nrm(ks[16], (DEPTH, D_FF, d), D_FF ** -0.5),
    }

def second_block(x, c, w_ada, b_ada, g_mix_pre, g_mix_post, g_ff_pre, g_ff_post, w_in, b_f,
              w_pool, pool_scale, conv_w, w_branch, w_out, w_ff1, w_ff2):
    for l in range(DEPTH):
        x = hybrid_layer_2(x, c, w_ada[l], b_ada[l], g_mix_pre[l], g_mix_post[l], g_ff_pre[l], g_ff_post[l],
                         w_in[l], b_f[l], w_pool[l], pool_scale[l], conv_w[l], w_branch[l], w_out[l],
                         w_ff1[l], w_ff2[l])
    return x


def setup_inputs(seed=0):
    out = dict(first_inputs(seed))
    for name, value in second_inputs(seed + 1).items():
        if name != "x":
            out[name + "_2"] = value
    return out


def reference(
    x, w_in, gmlp_w_s, gmlp_b_s, gmlp_ln_g, gmlp_ln_b, lam_q1, lam_k1, lam_q2, lam_k2,
    diff_subln_g, w_out, ln1_g, ln1_b, w_gu, w_down, ln2_g, ln2_b, c_2, w_ada_2, b_ada_2,
    g_mix_pre_2, g_mix_post_2, g_ff_pre_2, g_ff_post_2, w_in_2, b_f_2, w_pool_2, pool_scale_2,
    conv_w_2, w_branch_2, w_out_2, w_ff1_2, w_ff2_2,
):
    x = first_block(
        x, w_in, gmlp_w_s, gmlp_b_s, gmlp_ln_g, gmlp_ln_b, lam_q1, lam_k1, lam_q2, lam_k2,
        diff_subln_g, w_out, ln1_g, ln1_b, w_gu, w_down, ln2_g, ln2_b,
    )
    return second_block(
        x, c_2, w_ada_2, b_ada_2, g_mix_pre_2, g_mix_post_2, g_ff_pre_2, g_ff_post_2, w_in_2,
        b_f_2, w_pool_2, pool_scale_2, conv_w_2, w_branch_2, w_out_2, w_ff1_2, w_ff2_2,
    )


_drawn_inputs = setup_inputs


def setup_inputs(seed=0):
    import zlib

    import numpy as np

    out = dict(_drawn_inputs(seed))
    spreads = {}
    factors = {'gmlp_b_s': 3.56,
     'gmlp_ln_g': 7.953,
     'gmlp_ln_b': 29.178,
     'lam_q1': 57.376,
     'lam_k2': 98.488,
     'diff_subln_g': 3.348,
     'ln2_b': 2.683,
     'g_mix_post_2': 3.891,
     'g_ff_pre_2': 3.719,
     'g_ff_post_2': 4.078,
     'b_f_2': 64.0,
     'pool_scale_2': 3.222,
     'lam_k1': 5.859}
    for name, (base, spread) in spreads.items():
        noise = np.random.default_rng([zlib.crc32(name.encode()), seed]).standard_normal(out[name].shape)
        drawn = base * np.exp(spread * noise) if base else spread * noise
        out[name] = jnp.asarray(drawn.astype(out[name].dtype))
    for name, factor in factors.items():
        out[name] = (out[name] * factor).astype(out[name].dtype)
    return out
```

```python
from contextlib import ExitStack, nullcontext

import concourse.bass as bass
from concourse import mybir

F32 = mybir.dt.float32
F32R = mybir.dt.float32r
BF16 = mybir.dt.bfloat16
ALU = mybir.AluOpType
ACT = mybir.ActivationFunctionType
AX = mybir.AxisListType

P = 128
S = 1024
D = 1024
NB = S // P
KT = D // P
FH = 2816
FT = FH // P
FF = 4096
FFT = FF // P
NEG = -8e30
ALPHA = 2.0 ** 0.25
EPS_LN = 1e-5
EPS_RMS = 1e-6
TOPK = 256
TAKEN = -3.3e38
FORBIDDEN = -1e37
LAM_INIT = 0.8 - 0.6
N_CONSTS = 17
SLOPES = [2.0 ** (-2.0 * (h + 1)) for h in range(4)]
POOL_WINDOWS = (2, 4, 8, 16)

A_U, B_Q, B_V, C_Q, C_V, I_Q, I_K, I_W = 0, 512, 1536, 2048, 2560, 2816, 3072, 3104
V2, FL2, Z2, GL2 = 1024, 1536, 1544, 2568
N_ADA = 6 * D // P

FOUR = [(0, 1), (1, 1), (2, 1), (3, 1)]
BY_FEATURE = [(0, 0), (1, 1), (2, 2), (3, 3)]
TURN = [(b % 4, None) for b in range(NB)]
SCORE_UNITS = [(b, h) for b in range(2, NB) for h in range(8)]


def by_token_units(chunks):
    return [(0, None), (1, None), (2, None), (3, chunks - 1)]


def by_token_half(pairs, chunk):
    return [(p, None) for p in pairs[:3]] + [(pairs[3], chunk)]


DOWN1_PAIRS = [(0, 1, 2, 3), (0, 1, 2, 3)]
DOWN2_PAIRS = [(2, 3, 0, 1), (0, 1, 2, 3)]

STAGES = [
    ("turn_x", 1, [], TURN),
    ("cqk", 1, FOUR, BY_FEATURE),
    ("idx", 1, [(0, 1), (1, 1), (2, 4)], BY_FEATURE[:3]),
    ("cv", 1, [(s, 2) for s in range(4)], by_token_units(4)),
    ("auv", 1, FOUR, by_token_units(4)),
    ("turn_ws", 1, [], [(0, None)]),
    ("score", 1, [], [(n % 4, None) for n in range(len(SCORE_UNITS))]),
    ("gmlp", 1, [], [(0, None), (1, None)]),
    ("bqk", 2, FOUR, BY_FEATURE),
    ("bv", 1, FOUR, by_token_units(4)),
    ("ada", 1, [(j % 4, 1) for j in range(N_ADA)], []),
    ("turn_mix", 1, [], TURN),
    ("out1", 2, FOUR, by_token_units(4)),
    ("turn_x1", 1, [], TURN),
    ("ffn1", FT // 2, FOUR + FOUR[:2],
     BY_FEATURE + by_token_half(DOWN1_PAIRS[0], 4) + by_token_half(DOWN1_PAIRS[1], 5)),
    ("turn_h", 1, [], TURN),
    ("qk2", 2, FOUR, BY_FEATURE),
    ("v2", 1, FOUR, by_token_units(4)),
    ("fl2", 1, [(0, 1)], [(0, 0)]),
    ("z2", 2, FOUR, BY_FEATURE),
    ("turn_cum", 1, [], [(0, None)]),
    ("spread_cum", 1, [], TURN),
    ("pool", 1, [], [(0, None), (1, None)]),
    ("branch", KT, FOUR, [(0, 0), (1, 1), (2, 2), (3, None), (0, None), (1, 3)]),
    ("rows", 1, [], [(2, None), (3, None)]),
    ("out2", 2, FOUR, by_token_units(4)),
    ("turn_h2", 1, [], TURN),
    ("ffn2", FFT // 2, FOUR,
     BY_FEATURE[:2] + by_token_half(DOWN2_PAIRS[0], 2) + by_token_half(DOWN2_PAIRS[1], 3)),
    ("end", 1, [], []),
]
SPLIT = ("ffn1", "ffn2")


class Ledger:

    def __init__(self):
        self.iters, self.slots, self.units, self.base = {}, {}, {}, {}
        loads, uses, pairs, fulls = [0] * 4, [0] * 4, [0] * 4, [0] * 4
        parts, self.parts_base, self.high_base, highs = [1, 1], {}, {}, 0
        for name, n, slots, units in STAGES:
            self.iters[name], self.slots[name], self.units[name] = n, slots, units
            self.base[name] = (list(loads), list(uses), list(pairs), list(fulls))
            for s, dmas in slots:
                loads[s] += n * dmas
                uses[s] += n
            self.parts_base[name], self.high_base[name] = list(parts), highs
            if name in SPLIT:
                assert len(slots) % 2 == 0
                highs += n * len(slots)
                for c in range(len(slots)):
                    parts[c % 2] += n
            for p, chunk in units:
                pairs[p] += n
                fulls[p] += n * (chunk is None)

    def slot(self, stage, c):
        return self.slots[stage][c][0]

    def pair(self, stage, u):
        return self.units[stage][u][0]

    def loaded(self, stage, i, c):
        mine = self.slot(stage, c)
        dmas = [(s == mine) * d for s, d in self.slots[stage]]
        return (self.base[stage][0][mine] + sum(dmas[:c + 1])) * 16 + i * (sum(dmas) * 16)

    def slot_uses(self, stage, i, c):
        mine = self.slot(stage, c)
        used = [s == mine for s, _ in self.slots[stage]]
        return self.base[stage][1][mine] + sum(used[:c]) + i * sum(used)

    def pair_uses(self, stage, i, u):
        mine = self.pair(stage, u)
        used = [p == mine for p, _ in self.units[stage]]
        return self.base[stage][2][mine] + sum(used[:u]) + i * sum(used)

    def parts_uses(self, stage, i, c):
        return self.parts_base[stage][c % 2] + c // 2 + i * (len(self.slots[stage]) // 2)

    def full(self, stage, i, u):
        mine, chunk = self.units[stage][u]
        if chunk is not None and stage in SPLIT:
            return "parts_used", chunk % 2, self.parts_uses(stage, i, chunk) + 1
        if chunk is not None:
            return "weights_used", self.slot(stage, chunk), self.slot_uses(stage, i, chunk) + 1
        used = [p == mine and c is None for p, c in self.units[stage]]
        return "psum_full", mine, self.base[stage][3][mine] + sum(used[:u + 1]) + i * sum(used)


def loop(eng, n):
    return nullcontext(0) if n == 1 else eng.Fori(0, n)


def program(nc, t, out):
    L = Ledger()
    with ExitStack() as ctx:
        def sem(name):
            return ctx.enter_context(nc.semaphore(name))

        KB = 256
        END = 186 * KB
        arena = ctx.enter_context(nc.sbuf_tensor("arena", [P, END], F32))
        arena_base = nc.sbuf_base - END * 4

        def view(kb, *dims):
            n = 1
            for d in dims:
                n *= d
            a = arena[:, int(kb * KB):int(kb * KB) + n]
            names = "abcd"[:len(dims)]
            if len(dims) > 1:
                a = a.rearrange(f"p ({' '.join(names)}) -> p {' '.join(names)}",
                                **{x: d for x, d in zip(names[1:], dims[1:])})
            return a

        def rounded(name, kb, *dims):
            return nc.alloc_sbuf_tensor_at(name, [P, *dims], F32R, offset=arena_base + kb * 1024)

        def small(name, *shape):
            return ctx.enter_context(nc.sbuf_tensor(name, list(shape), F32))

        xT = view(0, KT, S)
        mix = view(0, NB, D)
        y1 = view(0, NB, D)
        x_tok = view(32, NB, D)
        bqkT = view(32, 8, S)
        mixT = view(32, KT, S)
        x1T_high, x1T_low = rounded("x1T_high", 32, KT, S), rounded("x1T_low", 64, KT, S)
        cqkT = view(64, 4, S)
        x_res = view(88, NB, D)
        au = view(80, NB, 256)
        av = view(88, NB, 256)
        mask_at = {b: sum(P * (c + 1) for c in range(2, b)) for b in range(2, NB)}
        mask_all = view(88, 2112).bitcast(BF16)
        mask = {b: mask_all[:, mask_at[b]:mask_at[b] + P * (b + 1)] for b in range(2, NB)}
        score_off = {b: int(141.5 * KB) + sum(P * (c + 1) for c in range(2, b)) for b in range(2, NB)}
        score = {b: arena[:, score_off[b]:score_off[b] + P * (b + 1)] for b in range(2, NB)}
        bv = view(97, NB, 512)
        cvw = view(113, NB, 264)
        iqT = view(121.5, 2, S)
        ikT = view(129.5, S)
        cbias = view(121.5, 2, S)
        logit = view(133.5, 2, S)
        relu = view(133.5, 2, S)
        prob = view(141.5, 4, S)
        probT = view(157.5, 2, NB, P)
        ws_tok = view(159, 4, P)
        v_sq = view(141.5, NB * 4, 64)
        dist = view(165.5, S)
        bias8 = view(169.5, 4, S)
        hid1_high, hid1_low = rounded("hid1_high", 96, 2, S), rounded("hid1_low", 104, 2, S)
        w1_high, w1_low = rounded("w1_high", 112, 2, 1024), rounded("w1_low", 120, 2, 1024)
        silu_t = view(152, 2, S)
        ln_g, ln_b = view(160, D), view(164, D)
        o_sq = view(133.5, 32, P)
        hT = view(32, KT, S)
        xhat = view(64, 2, D)
        qk2T = view(64, 8, S)
        z2T = view(96, 8, S)
        v2 = view(128, NB, 512)
        fl = view(144, S)
        brT = view(148, KT, S)
        pad_a = view(148, 16 + S)
        pad_b = view(152.25, 16 + S)
        ps_t = view(156.5, S)
        lsf_a = view(15, S)
        lsf_b = view(19, S)
        negcum = view(0, 8, S)
        logit2 = view(96, 2, S)
        prob2 = view(104, 2, S)
        probT2 = view(112, 2, NB, P)
        fbias = view(120, 2, S)
        sig = view(96, 3, S)
        mg = view(108, 2, S)
        mergedT = view(64, KT, S)
        y2 = view(96, NB, D)
        x2_res = view(128, NB, D)
        row_gain = view(160, D)
        diag = view(164, D)
        xhat2 = view(168, 2, D)
        h2T_high, h2T_low = rounded("h2T_high", 0, KT, S), rounded("h2T_low", 32, KT, S)
        shaped2 = nc.alloc_sbuf_tensor_at("shaped2", [P, 2, KT, P], F32, offset=arena_base + 128 * 1024)
        hid2_high, hid2_low = rounded("hid2_high", 128, 2, S), rounded("hid2_low", 136, 2, S)
        w2_high, w2_low = rounded("w2_high", 144, 2, 1024), rounded("w2_low", 152, 2, 1024)
        relu_t = view(160, 2, S)
        y3 = view(64, NB, D)
        row_gain2, diag2 = view(180, D), view(176, D)
        junks = [view(148, S), view(176, S), view(176, S), view(56, S)]

        ring = small("ring", P, 4, 1024)
        ident = small("ident", P, P)
        causal8 = small("causal8", P, P)
        wsT = small("wsT", P, 4, P)
        pool_w = small("pool_w", P, 2, P)
        misc = small("misc", P, 440)
        at = [0]

        def cut(n, *dims):
            a = misc[:, at[0]:at[0] + n]
            at[0] += n
            return a

        c_col, c_act, b_ada, mod = cut(KT), cut(KT), cut(N_ADA), cut(N_ADA)
        g_mix_pre, g_ff_pre, g_mix_post, g_ff_post = cut(KT), cut(KT), cut(KT), cut(KT)
        gain_m, gain_f, gate_m, gate_f = cut(KT), cut(KT), cut(KT), cut(KT)
        pscale, conv_w, b_f = cut(2), cut(6), cut(1)
        bs_col = cut(4)
        expsum, rowmin, rcp, coef = cut(8), cut(8), cut(8), cut(8)
        top8 = cut(48)
        lam_s, lam_e, neglam = cut(2), cut(2), cut(1)
        stats = cut(NB * 2)
        bn = cut(12)
        rstd, nmr, ssq = cut(NB), cut(NB), cut(NB)
        cumq8 = cut(64)
        o_ssq = cut(32)
        pool_inv = view(184, 2, 16)
        lam_v = view(163.75, 4, 64)
        vstat_lam = view(165, 2, 64)
        vstat = view(163.25, 3, 32)
        aln = view(161, 2, 256)
        subln = view(185.5, P)
        ones = view(185, P)
        selw = view(180, 8, P)

        PS = ctx.enter_context(nc.psum_tensor("PS", [P, 8, 512], F32))

        def pair(p):
            return PS[:, 2 * p:2 * p + 2, :]

        def flat(p):
            return pair(p).rearrange("p b n -> p (b n)")

        x2_dram = nc.dram_tensor("x2_spill", [S, D], F32).ap()

        weights_loaded = [sem(f"weights_loaded{s}") for s in range(4)]
        weights_used = [sem(f"weights_used{s}") for s in range(4)]
        parts_used = [sem(f"parts_used{q}") for q in range(2)]
        weights_high = sem("weights_high")
        psum_full = [sem(f"psum_full{p}") for p in range(4)]
        psum_free = [sem(f"psum_free{p}") for p in range(4)]
        tick = {e: sem(f"tick_{e}") for e in ("pe", "act", "dve", "pool", "sp")}
        dve_chain = sem("dve_chain")
        act_chain = sem("act_chain")
        pool_chain = sem("pool_chain")
        x_loaded = [sem(f"x_loaded{b}") for b in range(NB)]
        consts_loaded = sem("consts_loaded")
        ws_loaded, ws_masked = sem("ws_loaded"), sem("ws_masked")
        ident_made = sem("ident_made")
        dist_made = sem("dist_made")
        bias_made = sem("bias_made")
        lam_sums = sem("lam_sums")
        lam_exps = sem("lam_exps")
        lam_made = sem("lam_made")
        c_act_made = sem("c_act_made")
        mod_made = sem("mod_made")
        ada_done = sem("ada_done")
        v_normed = sem("v_normed")
        gmlp_var = sem("gmlp_var")
        gmlp_sqrt = sem("gmlp_sqrt")
        relu_made = sem("relu_made")
        score_added = sem("score_added")
        topk_done = sem("topk_done")
        cbias_made = sem("cbias_made")
        fbias_made = sem("fbias_made")
        o_var = sem("o_var")
        o_sqrt = sem("o_sqrt")
        mix_done = sem("mix_done")
        xres_loaded = sem("xres_loaded")
        ln_rows_loaded = [sem("ln1_rows_loaded"), sem("ln2_rows_loaded")]
        ln_var = [sem("ln1_var"), sem("ln2_var")]
        ln_sqrt = [sem("ln1_sqrt"), sem("ln2_sqrt")]
        ln_scaled = [sem("ln1_scaled"), sem("ln2_scaled")]
        ln_tile = [sem("ln1_tile"), sem("ln2_tile")]
        silu_made = sem("silu_made")
        hid_high, hid_made = ([sem(f"{n}{r}") for r in (1, 2)] for n in ("hid_high", "hid_made"))
        hid_squared = sem("hid_squared")
        y1_grown, y3_zeroed = sem("y1_grown"), sem("y3_zeroed")
        x1_high_made, h2_high_made, h2_shifted = sem("x1_high_made"), sem("h2_high_made"), sem("h2_shifted")
        rms_sum = [sem(f"rms_sum{r}") for r in range(4)]
        rms_var = [sem(f"rms_var{r}") for r in range(4)]
        rms_sqrt = [sem(f"rms_sqrt{r}") for r in range(4)]
        rms_rstd = [sem(f"rms_rstd{r}") for r in range(4)]
        x2_stored, x2_back = sem("x2_stored"), sem("x2_back")
        xhat_made = [sem("xhat_made"), sem("xhat2_made")]
        h_scaled = [sem("h_scaled"), sem("h2_scaled")]
        h_made = [sem("h_made"), sem("h2_made")]
        fl_exp, fl_ln, fl_done, cum_done = sem("fl_exp"), sem("fl_ln"), sem("fl_done"), sem("cum_done")
        selw_made = sem("selw_made")
        negcum_made = sem("negcum_made")
        pool_w_loaded, pool_w_zeroed = sem("pool_w_loaded"), sem("pool_w_zeroed")
        pooled = sem("pooled")
        br_bc_made = sem("br_bc_made")
        merged_step = sem("merged_step")
        topk_step = sem("topk_step")
        ones_made, counts_made = sem("ones_made"), sem("counts_made")
        ln_gained = [sem("ln1_gained"), sem("ln2_gained")]
        diag_made = sem("diag_made")
        y2_scaled, x3_made = sem("y2_scaled"), sem("x3_made")
        y3_scaled, out_made, out_stored = sem("y3_scaled"), sem("out_made"), sem("out_stored")

        def hold(name, eng, s, value):
            if isinstance(value, int):
                if value > 0:
                    eng.wait_ge(s, value)
            else:
                eng.wait_ge(s, value)
                eng.sem_inc(tick[name], 1)

        class Attention:
            def __init__(self, name, maps, units, q, k, v, dv, bias, dest, bufs, transposed, ada_from):
                self.name, self.maps, self.units = name, maps, units
                self.q, self.k, self.v, self.dv, self.bias, self.dest = q, k, v, dv, bias, dest
                self.logit, self.prob, self.probT = bufs
                self.n_prob = self.prob.shape[1]
                self.transposed, self.ada_from = transposed, ada_from
                self.out_banks = 2 if ada_from is None else 1
                self.scores_done = sem(name + "_scores_done")
                self.logits_made = sem(name + "_logits_made")
                self.probs_made = sem(name + "_probs_made")
                self.probs_ready = sem(name + "_probs_ready")
                self.turned = sem(name + "_turned")
                self.probsT_made = sem(name + "_probsT_made")
                self.out_done = sem(name + "_out_done")
                self.out_stored = sem(name + "_out_stored")

            def slot(self, u, m):
                return (u * self.maps + m) % self.n_prob

            def pe(self, pe):
                def scores(u):
                    h, b = self.units[u]
                    for m in range(self.maps):
                        n = u * self.maps + m
                        if n >= 2:
                            pe.wait_ge(self.logits_made, n - 1)
                        for c in range(0, P * (b + 1), 512):
                            w = min(512, P * (b + 1) - c)
                            mm = pe.matmul(PS[:, 2 * (n % 2) + c // 512, 0:w], self.q(h, m, b),
                                           self.k(h, m, c, w), start=True, stop=True)
                        mm.then_inc(self.scores_done, 1)

                def turn(u):
                    _, b = self.units[u]
                    pe.wait_ge(self.probs_ready, u + 1)
                    if u >= 1:
                        pe.wait_ge(self.probsT_made, u)
                    for s in range(b + 1):
                        mm = pe.transpose(PS[:, 4 + s // 4, (s % 4) * P:(s % 4 + 1) * P],
                                          self.prob[:, self.slot(u, 0), s * P:(s + 1) * P], ident[:, :])
                    mm.then_inc(self.turned, 1)

                def times_v(u):
                    h, b = self.units[u]
                    pe.wait_ge(self.probsT_made, u + 1)
                    if u >= self.out_banks:
                        pe.wait_ge(self.out_stored, u - self.out_banks + 1)
                    for s in range(b + 1):
                        pT = self.probT[:, u % 2, s, :]
                        if self.transposed:
                            lo = 64 * (h % 2)
                            mm = pe.matmul(PS[lo:lo + self.dv, 6 + u % self.out_banks, 0:P],
                                           self.v(h, s), pT, start=(s == 0), stop=(s == b))
                        else:
                            mm = pe.matmul(PS[:, 6 + u % self.out_banks, 0:self.dv],
                                           pT, self.v(h, s), start=(s == 0), stop=(s == b))
                    mm.then_inc(self.out_done, 1)

                scores(0)
                for u in range(len(self.units)):
                    if u + 1 < len(self.units):
                        scores(u + 1)
                    if self.ada_from is not None and self.ada_from + u < N_ADA:
                        ada(pe, self.ada_from + u)
                    if u >= 1:
                        times_v(u - 1)
                    turn(u)
                times_v(len(self.units) - 1)

            def act(self, act):
                def exps(u):
                    _, b = self.units[u]
                    N = P * (b + 1)
                    for m in range(self.maps):
                        n = u * self.maps + m
                        act.wait_ge(self.logits_made, n + 1)
                        back = self.n_prob // self.maps
                        if u >= back:
                            act.wait_ge(self.turned, u - back + 1)
                        act.activation(self.prob[:, self.slot(u, m), 0:N], self.logit[:, n % 2, 0:N],
                                       ACT.Exp, bias=rowmin[:, n % 8:n % 8 + 1], scale=-1.0,
                                       accum_out=expsum[:, n % 8:n % 8 + 1]).then_inc(self.probs_made, 1)

                def copy_turned(u):
                    _, b = self.units[u]
                    act.wait_ge(self.turned, u + 1)
                    if u >= 2:
                        act.wait_ge(self.out_done, u - 1)
                    act.copy(self.probT[:, u % 2, 0:b + 1, :].rearrange("p s n -> p (s n)"),
                             flat(2)[:, 0:P * (b + 1)]).then_inc(self.probsT_made, 1)

                exps(0)
                for u in range(len(self.units)):
                    if u + 1 < len(self.units):
                        exps(u + 1)
                    copy_turned(u)

            def dve(self, dve, link):
                def logits(u):
                    h, b = self.units[u]
                    N = P * (b + 1)
                    for m in range(self.maps):
                        n = u * self.maps + m
                        dve.wait_ge(self.scores_done, n + 1)
                        if n >= 2:
                            dve.wait_ge(self.probs_made, n - 1)
                        if self.bias is not None:
                            bias, s, value = self.bias(u)
                            if s is not None:
                                dve.wait_ge(s, value)
                        dve.tensor_tensor_reduce(out=self.logit[:, n % 2, 0:N],
                                                 in0=flat(n % 2)[:, 0:N], in1=bias, scale=-0.125,
                                                 scalar=3e38, op0=ALU.add, op1=ALU.min,
                                                 accum_out=rowmin[:, n % 8:n % 8 + 1]).then_inc(self.logits_made, 1)

                def combine(u):
                    _, b = self.units[u]
                    N = P * (b + 1)
                    n = u * self.maps
                    dve.wait_ge(self.probs_made, n + self.maps)
                    r = rcp[:, n % 8:n % 8 + 1]
                    if self.maps == 2:
                        dve.reciprocal(rcp[:, n % 8:n % 8 + 2], expsum[:, n % 8:n % 8 + 2]).then_inc(dve_chain, 1)
                        link()
                        dve.scalar_tensor_tensor(out=coef[:, n % 8:n % 8 + 1], in0=expsum[:, n % 8:n % 8 + 1],
                                                 scalar=neglam[:, 0:1], in1=rcp[:, n % 8 + 1:n % 8 + 2],
                                                 op0=ALU.mult, op1=ALU.mult).then_inc(dve_chain, 1)
                        link()
                        p0, p1 = (self.prob[:, self.slot(u, m), 0:N] for m in range(2))
                        dve.scalar_tensor_tensor(out=p0, in0=p1, scalar=coef[:, n % 8:n % 8 + 1], in1=p0,
                                                 op0=ALU.mult, op1=ALU.add).then_inc(self.probs_ready, 1)
                    elif self.transposed:
                        dve.reciprocal(r, expsum[:, n % 8:n % 8 + 1]).then_inc(dve_chain, 1)
                        link()
                        p0 = self.prob[:, self.slot(u, 0), 0:N]
                        dve.tensor_scalar(p0, p0, r, None, ALU.mult).then_inc(self.probs_ready, 1)
                    else:
                        dve.reciprocal(r, expsum[:, n % 8:n % 8 + 1]).then_inc(self.probs_ready, 1)

                def store(u):
                    h, b = self.units[u]
                    n = u * self.maps
                    dve.wait_ge(self.out_done, u + 1)
                    lo = 64 * (h % 2)
                    if self.transposed:
                        dve.tensor_copy(self.dest(h, b), PS[lo:lo + self.dv, 6 + u % self.out_banks, 0:P]
                                        ).then_inc(self.out_stored, 1)
                    else:
                        if self.maps == 1:
                            dve.wait_ge(self.probs_ready, u + 1)
                        dve.tensor_scalar(self.dest(h, b), PS[:, 6 + u % self.out_banks, 0:self.dv],
                                          rcp[:, n % 8:n % 8 + 1], None, ALU.mult).then_inc(self.out_stored, 1)

                logits(0)
                for u in range(len(self.units)):
                    if u + 1 < len(self.units):
                        logits(u + 1)
                    combine(u)
                    if u >= 1:
                        store(u - 1)
                store(len(self.units) - 1)
                dve.wait_ge(self.out_stored, len(self.units))

        heads4 = [(h, b) for h in range(4) for b in range(NB)]
        heads8 = [(h, b) for h in range(8) for b in range(NB)]

        def tok(b):
            return slice(b * P, (b + 1) * P)

        def b_bias(u):
            h, b = heads4[u]
            return bias8[:, h, P * (NB - 1 - b):S], bias_made, 4

        def c_bias(u):
            h, b = heads4[u]
            if b < 2:
                return bias8[:, h, P * (NB - 1 - b):S], None, 0
            k = h * (NB - 2) + b - 2
            return cbias[:, k % 2, 0:P * (b + 1)], cbias_made, k + 1

        def f_bias(u):
            return fbias[:, u % 2, 0:P * (heads8[u][1] + 1)], fbias_made, 2 * (u + 1)

        diff = Attention(
            "diff", 2, heads4,
            lambda h, m, b: bqkT[64 * m:64 * m + 64, h, tok(b)],
            lambda h, m, c, w: bqkT[64 * m:64 * m + 64, 4 + h, c:c + w],
            lambda h, s: bv[:, s, h * P:(h + 1) * P], P, b_bias,
            lambda h, b: mix[:, b, 256 + h * P:256 + (h + 1) * P],
            (logit, prob, probT), False, 0)
        sparse = Attention(
            "sparse", 1, heads4,
            lambda h, m, b: cqkT[64 * (h % 2):64 * (h % 2) + 64, h // 2, tok(b)],
            lambda h, m, c, w: cqkT[64 * (h % 2):64 * (h % 2) + 64, 2 + h // 2, c:c + w],
            lambda h, s: cvw[:, s, h * 64:(h + 1) * 64], 64, c_bias,
            lambda h, b: mix[:, b, 768 + h * 64:768 + (h + 1) * 64],
            (logit, prob, probT), False, 32)
        forget = Attention(
            "forget", 1, heads8,
            lambda h, m, b: qk2T[64 * (h % 2):64 * (h % 2) + 64, h // 2, tok(b)],
            lambda h, m, c, w: qk2T[64 * (h % 2):64 * (h % 2) + 64, 4 + h // 2, c:c + w],
            lambda h, s: v2[:, s, h * 64:(h + 1) * 64], 64, f_bias,
            lambda h, b: brT[64 * (h % 2):64 * (h % 2) + 64, h // 2, tok(b)],
            (logit2, prob2, probT2), True, None)

        def weights_here(pe, stage, i, c):
            hold("pe", pe, weights_loaded[L.slot(stage, c)], L.loaded(stage, i, c))

        def pair_here(pe, stage, i, u):
            hold("pe", pe, psum_free[L.pair(stage, u)], L.pair_uses(stage, i, u))

        def ada(pe, j):
            weights_here(pe, "ada", 0, j)
            w = ring[:, j % 4, :].rearrange("p (k n) -> p k n", k=KT)
            if j == 0:
                pe.wait_ge(c_act_made, 1)
            for k in range(KT):
                mm = pe.matmul(PS[:, 7, j:j + 1], w[:, k, :], c_act[:, k:k + 1], start=(k == 0), stop=(k == KT - 1))
            mm.then_inc(weights_used[j % 4], 1)

        def by_feature(pe, stage, source, width=P, before=None):
            with loop(pe, L.iters[stage]) as i:
                for c in range(len(L.slots[stage])):
                    s, p = L.slot(stage, c), L.pair(stage, c)
                    w = ring[:, s, 0:KT * width].rearrange("p (k n) -> p k n", k=KT)
                    weights_here(pe, stage, i, c)
                    pair_here(pe, stage, i, c)
                    for half in range(2):
                        for k in range(KT):
                            mm = pe.matmul(PS[0:width, 2 * p + half, :], w[:, k, :],
                                           source[:, k, half * 512:(half + 1) * 512],
                                           start=(k == 0), stop=(k == KT - 1))
                    mm.then_inc(weights_used[s], 1)

        def by_token(pe, stage, source, width=512):
            n = len(L.slots[stage])
            with loop(pe, L.iters[stage]) as i:
                for c in range(n):
                    s = L.slot(stage, c)
                    weights_here(pe, stage, i, c)
                    for kk in range(2):
                        k = 2 * c + kk
                        for b in range(NB):
                            if k == 0 and b % 2 == 0:
                                pair_here(pe, stage, i, b // 2)
                            last = k == 2 * n - 1 and b % 2 == 1
                            mm = pe.matmul(PS[:, b, 0:width], source[:, k, tok(b)],
                                           ring[:, s, kk * width:(kk + 1) * width],
                                           start=(k == 0), stop=(k == 2 * n - 1))
                            if last and b < NB - 1:
                                mm.then_inc(psum_full[b // 2], 1)
                    mm.then_inc(weights_used[s], 1)

        def split_here(pe, stage, i, c):
            hold("pe", pe, weights_used[L.slot(stage, c)], L.slot_uses(stage, i, c) + 1)

        def ffn(pe, r, stage, tiles, x_high, x_low, hid_parts, w_parts, down_pairs):
            w_high, w_low = w_parts
            hid_hi, hid_lo = hid_parts
            with pe.Fori(0, L.iters[stage]) as i:
                for c in range(tiles):
                    p = L.pair(stage, c)
                    split_here(pe, stage, i, c)
                    pair_here(pe, stage, i, c)
                    for half in range(2):
                        for k in range(KT):
                            for n, (w, x) in enumerate(((w_high, x_high), (w_high, x_low), (w_low, x_high))):
                                mm = pe.matmul(PS[:, 2 * p + half, :], w[:, c % 2, k * P:(k + 1) * P],
                                               x[:, k, half * 512:(half + 1) * 512],
                                               start=(k == 0 and n == 0), stop=(k == KT - 1 and n == 2))
                    mm.then_inc(parts_used[c % 2], 1)
                for half in range(2):
                    c = tiles + half
                    split_here(pe, stage, i, c)
                    for k in range(2):
                        if half == 0:
                            hold("pe", pe, hid_made[r], 2 * i + (3 + k))
                        for at, p in enumerate(down_pairs[half]):
                            if k == 0:
                                pair_here(pe, stage, i, tiles + 4 * half + at)
                            for b in (2 * p, 2 * p + 1):
                                for n, (h, w) in enumerate(((hid_hi, w_high), (hid_hi, w_low), (hid_lo, w_high))):
                                    mm = pe.matmul(PS[:, b, :], h[:, k, tok(b)], w[:, c % 2, k * 512:(k + 1) * 512],
                                                   start=(k == 0 and n == 0), stop=(k == 1 and n == 2))
                            if k == 1:
                                mm.then_inc(psum_full[p] if at < 3 else parts_used[c % 2], 1)

        def turn(pe, stage, source, ready):
            for b in range(NB):
                p = L.pair(stage, b)
                ready(b)
                pair_here(pe, stage, 0, b)
                for k in range(KT):
                    tile = au[:, b, :] if stage == "turn_mix" and k < 2 else source(b)
                    mm = pe.transpose(PS[:, 2 * p + k // 4, (k % 4) * P:(k % 4 + 1) * P],
                                      tile[:, k * P:(k + 1) * P], ident[:, :])
                mm.then_inc(psum_full[p], 1)

        def all_pairs_free(eng, stage):
            for p in range(4):
                eng.wait_ge(psum_free[p], L.base[stage][2][p])

        block = ctx.enter_context(nc.Block())

        @block.tensor
        def _(pe):
            for used in parts_used:
                pe.sem_inc(used, 1)
            pe.wait_ge(ident_made, 2)
            turn(pe, "turn_x", lambda b: x_tok[:, b, :], lambda b: pe.wait_ge(x_loaded[b], 16))
            all_pairs_free(pe, "cqk")
            by_feature(pe, "cqk", xT)
            by_feature(pe, "idx", xT)
            by_token(pe, "cv", xT, 264)
            by_token(pe, "auv", xT)
            pe.wait_ge(ws_masked, 1)
            pair_here(pe, "turn_ws", 0, 0)
            for g in range(4):
                mm = pe.transpose(PS[:, 0, g * P:(g + 1) * P], ws_tok[:, g, :], ident[:, :])
            mm.then_inc(psum_full[0], 1)
            pe.wait_ge(psum_free[0], L.pair_uses("idx", 0, 0) + 1)
            pe.wait_ge(psum_free[1], L.pair_uses("idx", 0, 1) + 1)
            pe.wait_ge(psum_free[2], L.pair_uses("idx", 0, 2) + 1)
            for n, (b, h) in enumerate(SCORE_UNITS):
                p = L.pair("score", n)
                lo = 32 * (h % 4)
                pair_here(pe, "score", 0, n)
                for c in range(0, P * (b + 1), 512):
                    w = min(512, P * (b + 1) - c)
                    mm = pe.matmul(PS[:, 2 * p + c // 512, 0:w], iqT[lo:lo + 32, h // 4, tok(b)],
                                   ikT[lo:lo + 32, c:c + w], start=True, stop=True)
                mm.then_inc(psum_full[p], 1)
            pe.wait_ge(v_normed, 1)
            for g in range(4):
                if g % 2 == 0:
                    pair_here(pe, "gmlp", 0, g // 2)
                mm = pe.matmul(PS[:, g, :], wsT[:, g, :], av[:, :, g * 64:(g + 1) * 64],
                               start=True, stop=True)
                if g % 2 == 1:
                    mm.then_inc(psum_full[g // 2], 1)
            by_feature(pe, "bqk", xT)
            by_token(pe, "bv", xT)
            all_pairs_free(pe, "ada")
            diff.pe(pe)
            sparse.pe(pe)
            hold("pe", pe, sparse.out_done, len(heads4))
            pe.sem_inc(ada_done, 1)
            turn(pe, "turn_mix", lambda b: mix[:, b, :],
                 lambda b: pe.wait_ge(mix_done, 1))
            all_pairs_free(pe, "out1")
            by_token(pe, "out1", mixT)
            turn(pe, "turn_x1", lambda b: y1[:, b, :], lambda b: pe.wait_ge(ln_tile[0], b + 1))
            all_pairs_free(pe, "ffn1")
            ffn(pe, 0, "ffn1", 4, x1T_high, x1T_low, (hid1_high, hid1_low), (w1_high, w1_low), DOWN1_PAIRS)
            turn(pe, "turn_h", lambda b: xhat[:, b % 2, :], lambda b: pe.wait_ge(xhat_made[0], b + 1))
            pe.wait_ge(h_made[0], NB)
            by_feature(pe, "qk2", hT)
            by_token(pe, "v2", hT)
            by_feature(pe, "fl2", hT, 8)
            by_feature(pe, "z2", hT)
            pe.wait_ge(cum_done, 1)
            pair_here(pe, "turn_cum", 0, 0)
            for b in range(NB):
                mm = pe.transpose(PS[:, 0, b * 8:b * 8 + 8], fl[0:8, tok(b)], ident[0:8, 0:8])
            mm.then_inc(psum_full[0], 1)
            pe.wait_ge(selw_made, 1)
            for h in range(8):
                p = L.pair("spread_cum", h)
                pair_here(pe, "spread_cum", 0, h)
                for half in range(2):
                    mm = pe.matmul(PS[:, 2 * p + half, :], selw[0:8, h, :], fl[0:8, half * 512:(half + 1) * 512],
                                   start=True, stop=True)
                mm.then_inc(psum_full[p], 1)
            pe.wait_ge(pool_w_loaded, 64)
            for g in range(2):
                pe.wait_ge(pooled, g + 1)
                pair_here(pe, "pool", 0, g)
                for half in range(2):
                    mm = pe.matmul(PS[:, 2 * g + half, :], pool_w[:, g, :], z2T[:, g, half * 512:(half + 1) * 512],
                                   start=True, stop=True)
                mm.then_inc(psum_full[g], 1)
            all_pairs_free(pe, "branch")
            forget.pe(pe)
            pe.wait_ge(forget.out_stored, len(heads8))
            pe.wait_ge(br_bc_made, 4)
            with loop(pe, KT) as i:
                for c in range(3):
                    p = L.pair("branch", c)
                    w = ring[:, c, :].rearrange("p (k n) -> p k n", k=KT)
                    weights_here(pe, "branch", i, c)
                    pair_here(pe, "branch", i, c)
                    for half in range(2):
                        for k in range(KT):
                            mm = pe.matmul(PS[:, 2 * p + half, :], w[:, k, :], hT[:, k, half * 512:(half + 1) * 512],
                                           start=(k == 0), stop=(k == KT - 1))
                    mm.then_inc(weights_used[c], 1)
                weights_here(pe, "branch", i, 3)
                w = ring[:, 3, :].rearrange("p (k n) -> p k n", k=KT)
                for br, ks in enumerate((range(0, 4), range(4, 6), range(6, 8))):
                    p = L.pair("branch", 3 + br)
                    pair_here(pe, "branch", i, 3 + br)
                    for half in range(2):
                        for k in ks:
                            mm = pe.matmul(PS[:, 2 * p + half, :], w[:, k, :], brT[:, k, half * 512:(half + 1) * 512],
                                           start=(k == ks[0]), stop=(k == ks[-1]))
                    mm.then_inc(weights_used[3] if br == 2 else psum_full[p], 1)
            pe.wait_ge(diag_made, KT * 2)
            pe.wait_ge(ones_made, 1)
            for r, dg in enumerate((diag, diag2)):
                p = L.pair("rows", r)
                pair_here(pe, "rows", 0, r)
                for half in range(2):
                    mm = pe.matmul(PS[:, 2 * p + half, :], ones[:, :], dg[:, half * 512:(half + 1) * 512],
                                   start=True, stop=True)
                mm.then_inc(psum_full[p], 1)
            pe.wait_ge(merged_step, 1 + 2 * KT)
            by_token(pe, "out2", mergedT)
            turn(pe, "turn_h2", lambda b: xhat2[:, b % 2, :], lambda b: pe.wait_ge(xhat_made[1], b + 1))
            pe.wait_ge(h_made[1], NB)
            ffn(pe, 1, "ffn2", 2, h2T_high, h2T_low, (hid2_high, hid2_low), (w2_high, w2_low), DOWN2_PAIRS)

        def unit_here(name, eng, stage, i, u):
            kind, n, value = L.full(stage, i, u)
            hold(name, eng, {"weights_used": weights_used, "parts_used": parts_used, "psum_full": psum_full}[kind][n],
                 value)

        def copy_turned(act, stage, dest):
            for b in range(NB):
                p = L.pair(stage, b)
                unit_here("act", act, stage, 0, b)
                act.copy(dest[:, :, tok(b)], flat(p).rearrange("p (k n) -> p k n", k=KT)).then_inc(psum_free[p], 1)

        def copy_features(act, stage, dest, at=0):
            n = len(L.units[stage])
            with loop(act, L.iters[stage]) as i:
                for c in range(n):
                    p = L.pair(stage, c)
                    unit_here("act", act, stage, i, c)
                    act.copy(dest[:, bass.ds(n * i + c + at, 1), :].rearrange("p a n -> p (a n)"), flat(p)
                             ).then_inc(psum_free[p], 1)

        def square_sums(act, r, source, waits):
            for b in range(NB):
                waits(b)
                act.activation(junks[r], source[:, b, :], ACT.Square, accum_out=ssq[:, b:b + 1]).then_inc(act_chain, 1)
                act_links[0] += 1
                act.wait_ge(act_chain, act_links[0])
            act.wait_ge(act_chain, act_links[0])
            act.sem_inc(rms_sum[r], 1)
            act.wait_ge(rms_var[r], 1)
            act.activation(rstd[:, :], rstd[:, :], ACT.Sqrt).then_inc(rms_sqrt[r], 1)

        act_links = [0]

        def layer_norm_act(act, r):
            act.wait_ge(ln_var[r], 1)
            act.activation(rstd[:, :], rstd[:, :], ACT.Sqrt).then_inc(ln_sqrt[r], 1)
            act.wait_ge(ln_sqrt[r], 2)
            for b in range(NB):
                act.activation(y1[:, b, :], y1[:, b, :], ACT.Identity, bias=nmr[:, b:b + 1],
                               scale=rstd[:, b:b + 1]).then_inc(ln_scaled[r], 1)

        def scale_rows(act, r, dest, source, stage):
            act.wait_ge(rms_rstd[2 * r], 1)
            for b in range(NB):
                if b >= 2:
                    unit_here("act", act, stage, 0, b - 2)
                act.activation(dest[:, b % 2, :], source[:, b, :], ACT.Copy, scale=rstd[:, b:b + 1]
                               ).then_inc(xhat_made[r], 1)

        @block.scalar
        def _(act):
            act.wait_ge(consts_loaded, 16 * N_CONSTS)
            act.activation(c_act[:, :], c_col[:, :], ACT.Silu).then_inc(c_act_made, 1)
            act.wait_ge(lam_sums, 2)
            act.activation(lam_e[:, :], lam_s[:, :], ACT.Exp).then_inc(lam_exps, 1)
            copy_turned(act, "turn_x", xT)
            copy_features(act, "cqk", cqkT)
            for c in range(3):
                p = L.pair("idx", c)
                unit_here("act", act, "idx", 0, c)
                act.copy(iqT[:, c, :] if c < 2 else ikT[:, :], flat(p)).then_inc(psum_free[p], 1)
            for p in range(4):
                unit_here("act", act, "cv", 0, p)
                act.copy(cvw[:, 2 * p:2 * p + 2, :], pair(p)[:, :, 0:264]).then_inc(psum_free[p], 1)
            for p in range(4):
                unit_here("act", act, "auv", 0, p)
                act.activation(au[:, 2 * p:2 * p + 2, :], pair(p)[:, :, 0:256], ACT.Gelu_apprx_tanh
                               ).then_inc(act_chain, 1)
                act_links[0] += 1
                act.activation(av[:, 2 * p:2 * p + 2, :], pair(p)[:, :, 256:512], ACT.Gelu_apprx_tanh
                               ).then_inc(psum_free[p], 1)
            act.wait_ge(act_chain, act_links[0])
            act.wait_ge(gmlp_var, 1)
            act.activation(vstat[:, 1, :], vstat[:, 1, :], ACT.Sqrt).then_inc(gmlp_sqrt, 1)
            for n, (b, h) in enumerate(SCORE_UNITS):
                p = L.pair("score", n)
                unit_here("act", act, "score", 0, n)
                if n >= 2:
                    act.wait_ge(score_added, n - 1)
                act.activation(relu[:, n % 2, 0:P * (b + 1)], flat(p)[:, 0:P * (b + 1)], ACT.Relu
                               ).then_inc(psum_free[p], 1)
            copy_features(act, "bqk", bqkT)
            for p in range(4):
                unit_here("act", act, "bv", 0, p)
                act.copy(bv[:, 2 * p:2 * p + 2, :], pair(p)).then_inc(psum_free[p], 1)
            act.wait_ge(topk_done, NB - 2)
            diff.act(act)
            act.wait_ge(o_var, 1)
            act.activation(o_ssq[:, :], o_ssq[:, :], ACT.Sqrt).then_inc(o_sqrt, 1)
            sparse.act(act)
            copy_turned(act, "turn_mix", mixT)
            layer_norm_act(act, 0)
            for b in range(NB):
                unit_here("act", act, "turn_x1", 0, b)
                act.copy(x1T_high[:, :, tok(b)], flat(L.pair("turn_x1", b)).rearrange("p (k n) -> p k n", k=KT)
                         ).then_inc(x1_high_made, 1)
            with act.Fori(0, FT // 2) as i:
                for j in range(2):
                    g, u = L.pair("ffn1", 2 * j), L.pair("ffn1", 2 * j + 1)
                    unit_here("act", act, "ffn1", i, 2 * j)
                    hold("act", act, hid_made[0], 2 * i + (j + 1))
                    act.activation(silu_t[:, j, :], flat(g), ACT.Silu).then_inc(psum_free[g], 1)
                    hold("act", act, psum_free[u], L.pair_uses("ffn1", i, 2 * j + 1) + 1)
                    act.copy(hid1_high[:, j, :], silu_t[:, j, :]).then_inc(hid_high[0], 1)
            layer_norm_act(act, 1)
            square_sums(act, 0, y1, lambda b: act.wait_ge(ln_tile[1], b + 1))
            scale_rows(act, 0, xhat, y1, "turn_h")
            copy_features(act, "qk2", qk2T)
            for p in range(4):
                unit_here("act", act, "v2", 0, p)
                act.copy(v2[:, 2 * p:2 * p + 2, :], pair(p)).then_inc(psum_free[p], 1)
            act.wait_ge(fl_exp, 1)
            act.activation(lsf_b[0:8, :], lsf_b[0:8, :], ACT.Exp, scale=-1.0).then_inc(act_chain, 1)
            act_links[0] += 1
            act.wait_ge(act_chain, act_links[0])
            act.activation(lsf_b[0:8, :], lsf_b[0:8, :], ACT.Ln, bias=1.0).then_inc(fl_ln, 1)
            copy_features(act, "z2", z2T)
            act.wait_ge(cum_done, 1)
            for h in range(8):
                p = L.pair("spread_cum", h)
                unit_here("act", act, "spread_cum", 0, h)
                act.activation(negcum[:, h, :], flat(p), ACT.Copy, scale=-8.0).then_inc(psum_free[p], 1)
            act.wait_ge(br_bc_made, 4)
            forget.act(act)
            with act.Fori(0, KT) as i:
                for c in range(3):
                    p, q = L.pair("branch", c), L.pair("branch", 3 + c)
                    unit_here("act", act, "branch", i, c)
                    hold("act", act, psum_free[q], L.pair_uses("branch", i, 3 + c))
                    act.activation(sig[:, c, :], flat(p), ACT.Sigmoid).then_inc(psum_free[p], 1)
            for r, dest in enumerate((row_gain, row_gain2)):
                p = L.pair("rows", r)
                unit_here("act", act, "rows", 0, r)
                act.copy(dest, flat(p)).then_inc(psum_free[p], 1)
            square_sums(act, 1, y2, lambda b: all_pairs_free(act, "turn_h2"))
            act.wait_ge(rms_rstd[1], 1)
            for b in range(NB):
                act.activation(y2[:, b, :], y2[:, b, :], ACT.Copy, scale=rstd[:, b:b + 1]).then_inc(y2_scaled, 1)
            act.wait_ge(y2_scaled, NB)
            square_sums(act, 2, y2, lambda b: act.wait_ge(x3_made, b + 1))
            act.wait_ge(rms_rstd[2], 1)
            for b in range(NB + 2):
                if b >= 2:
                    unit_here("act", act, "turn_h2", 0, b - 2)
                if b < NB:
                    act.activation(xhat2[:, b % 2, :], y2[:, b, :], ACT.Copy, scale=rstd[:, b:b + 1]
                                   ).then_inc(xhat_made[1], 1)
                if b >= 2:
                    act.wait_ge(h2_shifted, b - 1)
                    act.copy(h2T_high[:, :, tok(b - 2)], shaped2[:, b % 2, :, :]).then_inc(h2_high_made, 1)
            with act.Fori(0, FFT // 2) as i:
                for j in range(2):
                    p = L.pair("ffn2", j)
                    unit_here("act", act, "ffn2", i, j)
                    hold("act", act, hid_made[1], 2 * i + (j + 1))
                    act.activation(relu_t[:, j, :], flat(p), ACT.Relu).then_inc(psum_free[p], 1)
                    hold("act", act, hid_squared, 2 * i + (j + 1))
                    act.copy(hid2_high[:, j, :], relu_t[:, j, :]).then_inc(hid_high[1], 1)
            square_sums(act, 3, y3, lambda b: all_pairs_free(act, "end"))
            act.wait_ge(rms_rstd[3], 1)
            for b in range(NB):
                act.activation(y3[:, b, :], y3[:, b, :], ACT.Copy, scale=rstd[:, b:b + 1]).then_inc(y3_scaled, 1)

        links = [0]

        def add_scaled(dve, stage, dest, source):
            with dve.Fori(0, 2) as i:
                for p in range(4):
                    unit_here("dve", dve, stage, i, p)
                    where = (slice(None), slice(2 * p, 2 * p + 2), bass.ds(512 * i, 512))
                    dve.scalar_tensor_tensor(out=dest[where], in0=source[where], scalar=ALPHA, in1=pair(p),
                                             op0=ALU.mult, op1=ALU.add).then_inc(psum_free[p], 1)

        def low_hidden(dve, r, i, j, hidden, hid_parts):
            hold("dve", dve, hid_high[r], 2 * i + (j + 1))
            dve.tensor_tensor(hid_parts[1][:, j, :], hidden[:, j, :], hid_parts[0][:, j, :].bitcast(F32), ALU.subtract
                              ).then_inc(hid_made[r], 1)

        def add_halves(dve, stage, i, tiles, dest, down_pairs):
            for half in range(2):
                for at, p in enumerate(down_pairs[half]):
                    unit_here("dve", dve, stage, i, tiles + 4 * half + at)
                    where = dest[:, 2 * p:2 * p + 2, half * 512:(half + 1) * 512]
                    dve.tensor_tensor(where, where, pair(p), ALU.add).then_inc(psum_free[p], 1)

        def layer_norm_dve(dve, do, link, r):
            all_pairs_free(dve, ("turn_x1", "turn_h")[r])
            for b in range(NB):
                for half in range(2):
                    do(dve.bn_stats(bn[:, 6 * half:6 * half + 6], y1[:, b, half * 512:(half + 1) * 512]))
                do(dve.bn_aggr(stats[:, 2 * b:2 * b + 2], bn[:, :]))
            st = stats[:, :].rearrange("p (b c) -> p b c", c=2)
            dve.tensor_scalar(rstd[:, :], st[:, :, 1], EPS_LN, None, ALU.add).then_inc(ln_var[r], 1)
            dve.wait_ge(ln_sqrt[r], 1)
            do(dve.reciprocal(rstd[:, :], rstd[:, :]))
            dve.scalar_tensor_tensor(out=nmr[:, :], in0=st[:, :, 0], scalar=-1.0, in1=rstd[:, :],
                                     op0=ALU.mult, op1=ALU.mult).then_inc(ln_sqrt[r], 1)
            dve.wait_ge(ln_rows_loaded[r], 32)
            for b in range(NB):
                dve.wait_ge(ln_scaled[r], b + 1)
                dve.tensor_tensor(y1[:, b, :], y1[:, b, :], ln_g, ALU.mult).then_inc(ln_gained[r], 1)

        def rms_dve(dve, do, r):
            dve.wait_ge(rms_sum[r], 1)
            dve.tensor_scalar(rstd[:, :], ssq[:, :], 1.0 / D, EPS_RMS, ALU.mult, ALU.add).then_inc(rms_var[r], 1)
            dve.wait_ge(rms_sqrt[r], 1)
            dve.reciprocal(rstd[:, :], rstd[:, :]).then_inc(rms_rstd[r], 1)

        def modulate(dve, stage, dest, gain, r):
            for b in range(NB):
                p = L.pair(stage, b)
                unit_here("dve", dve, stage, 0, b)
                dve.tensor_tensor(dest[:, :, tok(b)], flat(p).rearrange("p (k n) -> p k n", k=KT),
                                  gain[:, :].unsqueeze(2).to_broadcast([P, KT, P]), ALU.mult).then_inc(psum_free[p], 1)

        @block.vector
        def _(dve):
            def link():
                links[0] += 1
                dve.wait_ge(dve_chain, links[0])

            def do(ins):
                ins.then_inc(dve_chain, 1)
                link()

            dve.wait_ge(dist_made, 1)
            do(dve.scalar_tensor_tensor(out=dist, in0=dist, scalar=-1.0, in1=dist, op0=ALU.mult, op1=ALU.max))
            for h in range(4):
                do(dve.tensor_scalar(bias8[:, h, :], dist, -8.0 * SLOPES[h], None, ALU.mult))
                dve.memset(bias8[0:64, h, S - 64:S], NEG).then_inc(bias_made, 1)
            dve.wait_ge(consts_loaded, 16 * N_CONSTS)
            for j in range(2):
                dve.tensor_tensor_reduce(out=vstat_lam[:, j, :], in0=lam_v[:, 2 * j, :], in1=lam_v[:, 2 * j + 1, :],
                                         scale=1.0, scalar=0.0, op0=ALU.mult, op1=ALU.add,
                                         accum_out=lam_s[:, j:j + 1]).then_inc(lam_sums, 1)
            dve.wait_ge(lam_exps, 1)
            do(dve.tensor_tensor(neglam[:, :], lam_e[:, 1:2], lam_e[:, 0:1], ALU.subtract))
            do(dve.tensor_scalar(neglam[:, :], neglam[:, :], -LAM_INIT, None, ALU.add))
            for p in range(4):
                dve.wait_ge(psum_free[p], L.pair_uses("cv", 0, p) + 1)
            do(dve.tensor_scalar(cvw[:, :, 256:264], cvw[:, :, 256:264], 1.0 / 16, None, ALU.mult))
            for p in range(4):
                dve.wait_ge(psum_free[p], L.pair_uses("auv", 0, p) + 1)
            unit_here("dve", dve, "turn_ws", 0, 0)
            dve.tensor_copy(wsT[:, :, :].rearrange("p g n -> p (g n)"), PS[:, 0, :]).then_inc(psum_free[0], 1)
            vg = av.rearrange("p b (g c) -> p (b g) c", c=64)

            def over(stat):
                return stat.unsqueeze(2).to_broadcast([P, NB * 4, 64])

            do(dve.tensor_reduce(vstat[:, 0, :], vg, AX.X, ALU.add))
            do(dve.tensor_scalar(vstat[:, 0, :], vstat[:, 0, :], 1.0 / 64, None, ALU.mult))
            do(dve.tensor_tensor(vg, vg, over(vstat[:, 0, :]), ALU.subtract))
            do(dve.tensor_tensor(v_sq, vg, vg, ALU.mult))
            do(dve.tensor_reduce(vstat[:, 1, :], v_sq, AX.X, ALU.add))
            dve.tensor_scalar(vstat[:, 1, :], vstat[:, 1, :], 1.0 / 64, EPS_LN, ALU.mult, ALU.add
                              ).then_inc(gmlp_var, 1)
            dve.wait_ge(gmlp_sqrt, 1)
            do(dve.reciprocal(vstat[:, 2, :], vstat[:, 1, :]))
            do(dve.tensor_tensor(vg, vg, over(vstat[:, 2, :]), ALU.mult))
            do(dve.tensor_tensor(av, av, aln[:, 0:1, :].to_broadcast([P, NB, 256]), ALU.mult))
            dve.tensor_tensor(av, av, aln[:, 1:2, :].to_broadcast([P, NB, 256]), ALU.add).then_inc(v_normed, 1)
            for n, (b, h) in enumerate(SCORE_UNITS):
                N = P * (b + 1)
                dve.wait_ge(psum_free[L.pair("score", n)], L.pair_uses("score", 0, n) + 1)
                wcol = cvw[:, b, 256 + h:257 + h]
                if h == 0:
                    dve.tensor_scalar(score[b], relu[:, n % 2, 0:N], wcol, None, ALU.mult).then_inc(score_added, 1)
                else:
                    dve.wait_ge(score_added, n)
                    dve.scalar_tensor_tensor(out=score[b], in0=relu[:, n % 2, 0:N], scalar=wcol, in1=score[b],
                                             op0=ALU.mult, op1=ALU.add).then_inc(score_added, 1)
            for g in range(4):
                if g % 2 == 0:
                    unit_here("dve", dve, "gmlp", 0, g // 2)
                ug = au[:, :, g * 64:(g + 1) * 64]
                ins = dve.scalar_tensor_tensor(out=ug, in0=PS[:, g, :].rearrange("p (b c) -> p b c", c=64),
                                               scalar=bs_col[:, g:g + 1], in1=ug, op0=ALU.add, op1=ALU.mult)
                ins.then_inc(psum_free[g // 2] if g % 2 else dve_chain, 1)
                if g % 2 == 0:
                    link()
            dve.wait_ge(score_added, len(SCORE_UNITS))
            blocks = range(2, NB)
            for b in blocks:
                dve.memset(score[b][0:64, P * b + 64:P * b + P], FORBIDDEN).then_inc(topk_step, 1)
            nb = len(blocks)
            with dve.Fori(0, TOPK // 8) as i:
                for b in blocks:
                    hold("dve", dve, topk_step, 2 * nb * i + b - 1)
                    dve.max(top8[:, 8 * (b - 2):8 * (b - 1)], score[b]).then_inc(topk_step, 1)
                for b in blocks:
                    hold("dve", dve, topk_step, nb + 2 * nb * i + b - 1)
                    dve.match_replace(out=score[b], in_to_replace=top8[:, 8 * (b - 2):8 * (b - 1)],
                                      in_values=score[b], imm_value=TAKEN).then_inc(topk_step, 1)
            dve.wait_ge(topk_step, nb + 2 * nb * (TOPK // 8))
            for b in blocks:
                dve.tensor_scalar(mask[b], score[b], -2e38, NEG, ALU.is_gt, ALU.mult).then_inc(topk_done, 1)
            for p in range(4):
                dve.wait_ge(psum_free[p], L.pair_uses("bv", 0, p) + 1)
            dve.wait_ge(topk_done, nb)
            diff.dve(dve, link)
            o_heads = [mix[:, b, 256:768].rearrange("p (h e) -> p h e", e=P) for b in range(NB)]
            for half in range(2):
                for b in range(4 * half, 4 * half + 4):
                    do(dve.tensor_tensor(o_sq[:, 4 * (b % 4):4 * (b % 4) + 4, :], o_heads[b], o_heads[b], ALU.mult))
                do(dve.tensor_reduce(o_ssq[:, 16 * half:16 * half + 16], o_sq[:, 0:16, :], AX.X, ALU.add))
            dve.tensor_scalar(o_ssq[:, :], o_ssq[:, :], 1.0 / P, EPS_LN, ALU.mult, ALU.add).then_inc(o_var, 1)
            dve.wait_ge(o_sqrt, 1)
            do(dve.reciprocal(o_ssq[:, :], o_ssq[:, :]))
            do(dve.tensor_scalar(o_ssq[:, :], o_ssq[:, :], 1.0 - LAM_INIT, None, ALU.mult))
            for b in range(NB):
                do(dve.tensor_tensor(o_heads[b], o_heads[b],
                                     o_ssq[:, 4 * b:4 * b + 4].unsqueeze(2).to_broadcast([P, 4, P]), ALU.mult))
                do(dve.tensor_tensor(o_heads[b], o_heads[b],
                                     subln.unsqueeze(1).to_broadcast([P, 4, P]), ALU.mult))
            sparse.dve(dve, link)
            dve.wait_ge(ada_done, 1)
            do(dve.tensor_tensor(mod[:, :], PS[:, 7, 0:N_ADA], b_ada[:, :], ALU.add))
            dve.sem_inc(mix_done, 1)
            for gain, k, g in ((gain_m, 1, g_mix_pre), (gain_f, 4, g_ff_pre)):
                do(dve.scalar_tensor_tensor(out=gain[:, :], in0=mod[:, KT * k:KT * k + KT], scalar=1.0, in1=g[:, :],
                                            op0=ALU.add, op1=ALU.mult))
            for gate, k, g in ((gate_m, 2, g_mix_post), (gate_f, 5, g_ff_post)):
                do(dve.tensor_tensor(gate[:, :], mod[:, KT * k:KT * k + KT], g[:, :], ALU.mult))
            dve.sem_inc(mod_made, 1)
            dve.wait_ge(xres_loaded, 16)
            add_scaled(dve, "out1", y1, x_res)
            layer_norm_dve(dve, do, link, 0)
            for b in range(NB):
                p = L.pair("turn_x1", b)
                dve.wait_ge(x1_high_made, b + 1)
                dve.tensor_tensor(x1T_low[:, :, tok(b)], flat(p).rearrange("p (k n) -> p k n", k=KT),
                                  x1T_high[:, :, tok(b)].bitcast(F32), ALU.subtract).then_inc(psum_free[p], 1)
            for b in range(NB):
                dve.tensor_scalar(y1[:, b, :], y1[:, b, :], ALPHA, None, ALU.mult).then_inc(y1_grown, 1)
            dve.wait_ge(y1_grown, NB)
            dve.sem_inc(hid_made[0], 2)
            with dve.Fori(0, FT // 2) as i:
                for j in range(2):
                    u = L.pair("ffn1", 2 * j + 1)
                    unit_here("dve", dve, "ffn1", i, 2 * j + 1)
                    hold("dve", dve, psum_free[L.pair("ffn1", 2 * j)], L.pair_uses("ffn1", i, 2 * j) + 1)
                    dve.tensor_tensor(silu_t[:, j, :], silu_t[:, j, :], flat(u), ALU.mult).then_inc(psum_free[u], 1)
                    low_hidden(dve, 0, i, j, silu_t, (hid1_high, hid1_low))
                add_halves(dve, "ffn1", i, 4, y1, DOWN1_PAIRS)
            layer_norm_dve(dve, do, link, 1)
            rms_dve(dve, do, 0)
            modulate(dve, "turn_h", hT, gain_m, 0)
            unit_here("dve", dve, "fl2", 0, 0)
            dve.wait_ge(x2_stored, 16)
            dve.tensor_scalar(lsf_a[0:8, :], flat(0)[0:8, :], b_f[0:8, 0:1], None, ALU.add).then_inc(psum_free[0], 1)
            dve.wait_ge(psum_free[0], L.pair_uses("fl2", 0, 0) + 1)
            dve.scalar_tensor_tensor(out=lsf_b[0:8, :], in0=lsf_a[0:8, :], scalar=-1.0, in1=lsf_a[0:8, :],
                                     op0=ALU.mult, op1=ALU.max).then_inc(fl_exp, 1)
            dve.wait_ge(fl_ln, 1)
            do(dve.scalar_tensor_tensor(out=lsf_a[0:8, :], in0=lsf_a[0:8, :], scalar=0.0, in1=lsf_b[0:8, :],
                                        op0=ALU.min, op1=ALU.subtract))
            do(dve.memset(lsf_b[0:8, :], 1.0))
            dve.tensor_tensor_scan(fl[0:8, :], lsf_b[0:8, :], lsf_a[0:8, :], 0.0, ALU.mult, ALU.add
                                   ).then_inc(cum_done, 1)
            unit_here("dve", dve, "turn_cum", 0, 0)
            dve.tensor_scalar(cumq8[:, :], PS[:, 0, 0:64], 8.0, None, ALU.mult).then_inc(psum_free[0], 1)
            dve.wait_ge(counts_made, 2)
            for g in range(2):
                for half in range(2):
                    r = slice(64 * half, 64 * half + 64)
                    do(dve.tensor_scalar(pool_inv[r, g, :], pool_inv[r, g, :], float(POOL_WINDOWS[2 * g + half]), None,
                                         ALU.min))
            do(dve.reciprocal(pool_inv, pool_inv))
            for p in range(4):
                dve.wait_ge(psum_free[p], L.pair_uses("z2", 1, p) + 1)
            do(dve.memset(pad_a[:, 0:16], 0.0))
            do(dve.memset(pad_b[:, 0:16], 0.0))
            for g in range(2):
                do(dve.tensor_copy(pad_a[:, 16:16 + S], z2T[:, g, :]))
                src, dst, shift = pad_a, pad_b, 1
                for _ in range(1 + 2 * g):
                    do(dve.tensor_tensor(dst[:, 16:16 + S], src[:, 16:16 + S], src[:, 16 - shift:16 - shift + S], ALU.add))
                    src, dst, shift = dst, src, 2 * shift
                do(dve.tensor_tensor(dst[64:128, 16:16 + S], src[64:128, 16:16 + S],
                                     src[64:128, 16 - shift:16 - shift + S], ALU.add))
                for half, sums in enumerate((src, dst)):
                    r = slice(64 * half, 64 * half + 64)
                    w = POOL_WINDOWS[2 * g + half]
                    do(dve.tensor_tensor(sums[r, 16:32], sums[r, 16:32], pool_inv[r, g, :], ALU.mult))
                    do(dve.tensor_tensor(z2T[r, g, 0:16], sums[r, 16:32], z2T[r, g, 0:16], ALU.subtract))
                    do(dve.scalar_tensor_tensor(out=z2T[r, g, 16:S], in0=sums[r, 32:16 + S], scalar=1.0 / w,
                                                in1=z2T[r, g, 16:S], op0=ALU.mult, op1=ALU.subtract))
                dve.sem_inc(pooled, 1)
            for g in range(2):
                do(dve.tensor_tensor(pad_a[:, 16:16 + S], z2T[:, 6 + g, :], z2T[:, 2 + g, :], ALU.mult))
                do(dve.tensor_scalar(ps_t, pad_a[:, 16:16 + S], conv_w[:, 4 + g:5 + g], None, ALU.mult))
                for tap in (1, 0):
                    back = 2 - tap
                    do(dve.scalar_tensor_tensor(out=ps_t, in0=pad_a[:, 16 - back:16 - back + S],
                                                scalar=conv_w[:, 2 * tap + g:2 * tap + g + 1], in1=ps_t,
                                                op0=ALU.mult, op1=ALU.add))
                do(dve.tensor_tensor(brT[:, 6 + g, :], ps_t, z2T[:, 4 + g, :], ALU.mult))
                dve.sem_inc(br_bc_made, 1)
            for g in range(2):
                unit_here("dve", dve, "pool", 0, g)
                dve.tensor_scalar(brT[:, 4 + g, :], flat(g), pscale[:, g:g + 1], None, ALU.mult
                                  ).then_inc(psum_free[g], 1)
                dve.wait_ge(psum_free[g], L.pair_uses("pool", 0, g) + 1)
                dve.sem_inc(br_bc_made, 1)
            forget.dve(dve, link)
            dve.sem_inc(merged_step, 1)
            with dve.Fori(0, KT) as i:
                for c in range(3):
                    p, q = L.pair("branch", c), L.pair("branch", 3 + c)
                    unit_here("dve", dve, "branch", i, 3 + c)
                    hold("dve", dve, psum_free[p], L.pair_uses("branch", i, c) + 1)
                    hold("dve", dve, merged_step, 2 * i + 1 + (c == 2))
                    dve.tensor_tensor(mg[:, min(c, 1), :], sig[:, c, :], flat(q), ALU.mult).then_inc(psum_free[q], 1)
                    if c == 0:
                        continue
                    hold("dve", dve, psum_free[q], L.pair_uses("branch", i, 3 + c) + 1)
                    dest = mg[:, 0, :] if c == 1 else mergedT[:, bass.ds(i, 1), :].rearrange("p a n -> p (a n)")
                    dve.tensor_tensor(dest, mg[:, 0, :], mg[:, 1, :], ALU.add).then_inc(merged_step, 1)
            for dg, gate in ((diag, gate_m), (diag2, gate_f)):
                for k in range(KT):
                    dve.tensor_scalar(dg[:, k * P:(k + 1) * P], ident[:, :], gate[:, k:k + 1], None, ALU.mult
                                      ).then_inc(diag_made, 1)
            with dve.Fori(0, 2) as i:
                for p in range(4):
                    unit_here("dve", dve, "out2", i, p)
                    dve.tensor_copy(y2[:, 2 * p:2 * p + 2, bass.ds(512 * i, 512)], pair(p)).then_inc(psum_free[p], 1)
            rms_dve(dve, do, 1)
            dve.wait_ge(x2_back, 16)
            for r in range(2):
                dve.wait_ge(psum_free[L.pair("rows", r)], L.pair_uses("rows", 0, r) + 1)
            for b in range(NB):
                dve.wait_ge(y2_scaled, b + 1)
                do(dve.tensor_tensor(y2[:, b, :], y2[:, b, :], row_gain, ALU.mult))
                dve.tensor_tensor(y2[:, b, :], y2[:, b, :], x2_res[:, b, :], ALU.add).then_inc(x3_made, 1)
            rms_dve(dve, do, 2)
            for b in range(NB + 1):
                if b < NB:
                    p = L.pair("turn_h2", b)
                    unit_here("dve", dve, "turn_h2", 0, b)
                    if b >= 2:
                        dve.wait_ge(h_made[1], b - 1)
                    dve.tensor_tensor(shaped2[:, b % 2, :, :], flat(p).rearrange("p (k n) -> p k n", k=KT),
                                      gain_f[:, :].unsqueeze(2).to_broadcast([P, KT, P]), ALU.mult
                                      ).then_inc(psum_free[p], 1)
                if b >= 1:
                    dve.wait_ge(h2_high_made, b)
                    dve.tensor_tensor(h2T_low[:, :, tok(b - 1)], shaped2[:, (b - 1) % 2, :, :],
                                      h2T_high[:, :, tok(b - 1)].bitcast(F32), ALU.subtract).then_inc(h_made[1], 1)
            dve.wait_ge(y3_zeroed, 1)
            dve.sem_inc(hid_made[1], 2)
            with dve.Fori(0, FFT // 2) as i:
                for j in range(2):
                    hold("dve", dve, psum_free[L.pair("ffn2", j)], L.pair_uses("ffn2", i, j) + 1)
                    dve.tensor_tensor(relu_t[:, j, :], relu_t[:, j, :], relu_t[:, j, :], ALU.mult
                                      ).then_inc(hid_squared, 1)
                    low_hidden(dve, 1, i, j, relu_t, (hid2_high, hid2_low))
                add_halves(dve, "ffn2", i, 2, y3, DOWN2_PAIRS)
            rms_dve(dve, do, 3)
            for b in range(NB):
                dve.wait_ge(y3_scaled, b + 1)
                do(dve.tensor_tensor(y3[:, b, :], y3[:, b, :], row_gain2, ALU.mult))
                dve.tensor_tensor(y3[:, b, :], y3[:, b, :], y2[:, b, :], ALU.add).then_inc(out_made, 1)

        def shift(pool, r, dest, col, stage):
            for b in range(NB):
                p = L.pair(stage, b)
                pool.wait_ge(psum_free[p], L.pair_uses(stage, 0, b) + 1)
                pool.tensor_tensor(dest[:, :, tok(b)], dest[:, :, tok(b)],
                                   col.unsqueeze(2).to_broadcast([P, KT, P]), ALU.add).then_inc(h_made[r], 1)

        def split_weights(pool, stage, w_high, w_low):
            n = len(L.slots[stage])
            with loop(pool, L.iters[stage]) as i:
                for c in range(n):
                    s = L.slot(stage, c)
                    hold("pool", pool, weights_loaded[s], L.loaded(stage, i, c))
                    hold("pool", pool, parts_used[c % 2], L.parts_uses(stage, i, c))
                    pool.tensor_scalar(w_high[:, c % 2, :], ring[:, s, :], 1.0, 1.0, ALU.mult, ALU.mult
                                       ).then_inc(weights_high, 1)
                    hold("pool", pool, weights_high, L.high_base[stage] + n * i + (c + 1))
                    pool.tensor_tensor(w_low[:, c % 2, :], ring[:, s, :], w_high[:, c % 2, :].bitcast(F32),
                                       ALU.subtract).then_inc(weights_used[s], 1)

        @block.gpsimd
        def _(pool):
            loads = 0

            def load(dst, src):
                nonlocal loads
                with nc.allow_non_contiguous_dma(reason="small constants"):
                    pool.dma_start(dst, src).then_inc(consts_loaded, 16)
                loads += 1

            def column(name, width=P):
                return t[name].rearrange("a (k p) -> p (a k)", p=width)

            links = [0]

            def do(ins):
                links[0] += 1
                ins.then_inc(pool_chain, 1)
                pool.wait_ge(pool_chain, links[0])

            do(pool.memset(ident[:, :], 0.0))
            pool.affine_select(out=ident[:, :], in_=ident[:, :], compare_op=ALU.not_equal, fill=1.0, base=0,
                               pattern=[[-1, P]], channel_multiplier=1).then_inc(ident_made, 1)
            do(pool.memset(causal8[:, :], 0.0))
            pool.affine_select(out=causal8[:, :], in_=causal8[:, :], compare_op=ALU.is_ge, fill=NEG, base=0,
                               pattern=[[-1, P]], channel_multiplier=1).then_inc(ident_made, 1)
            pool.iota(dist, pattern=[[-1, S]], base=S - P, channel_multiplier=1,
                      allow_small_or_imprecise_dtypes=True).then_inc(dist_made, 1)
            load(c_col[:, :], column("c_2"))
            load(b_ada[:, :], column("b_ada_2"))
            for dst, name in ((g_mix_pre, "g_mix_pre_2"), (g_ff_pre, "g_ff_pre_2"), (g_mix_post, "g_mix_post_2"),
                              (g_ff_post, "g_ff_post_2"), (pscale, "pool_scale_2")):
                load(dst[:, :], column(name))
            load(conv_w[:, :], t["conv_w_2"].rearrange("a t (g p) -> p (a t g)", p=P))
            load(b_f[0:8, :], t["b_f_2"].rearrange("a h -> h a"))
            load(bs_col[:, :], t["gmlp_b_s"].rearrange("a g n -> n (a g)"))
            for j, name in enumerate(("lam_q1", "lam_k1", "lam_q2", "lam_k2")):
                load(lam_v[:, j, :], t[name].to_broadcast([P, 64]))
            load(subln, t["diff_subln_g"].to_broadcast([P, P]))
            for j, name in enumerate(("gmlp_ln_g", "gmlp_ln_b")):
                load(aln[:, j, :], t[name].rearrange("a g c -> a (g c)").to_broadcast([P, 256]))
            assert loads == N_CONSTS
            pool.dma_start(ws_tok, t["gmlp_w_s"].rearrange("a g t s -> t (a g) s")).then_inc(ws_loaded, 16)
            pool.wait_ge(ws_loaded, 16)
            pool.memset(ws_tok[0:64, :, 64:128], 0.0).then_inc(ws_masked, 1)
            pool.memset(pool_w[:, :, :], 0.0).then_inc(pool_w_zeroed, 1)
            pool.wait_ge(pool_w_zeroed, 1)
            for g in range(4):
                r = slice(64 * (g % 2), 64 * (g % 2) + 64)
                pool.dma_start(pool_w[r, g // 2, r], t["w_pool_2"][0, g]).then_inc(pool_w_loaded, 16)
            pool.wait_ge(topk_done, NB - 2)
            k = 0
            for u, (h, b) in enumerate(heads4):
                if b < 2:
                    continue
                if k >= 2:
                    prev = [v for v, (_, bb) in enumerate(heads4) if bb >= 2][k - 2]
                    pool.wait_ge(sparse.logits_made, prev + 1)
                pool.tensor_tensor(cbias[:, k % 2, 0:P * (b + 1)], bias8[:, h, P * (NB - 1 - b):S], mask[b], ALU.add
                                   ).then_inc(cbias_made, 1)
                k += 1
            pool.wait_ge(sparse.out_stored, len(heads4))
            pool.dma_start(x_res, t["x"][0].rearrange("(b p) d -> p b d", p=P)).then_inc(xres_loaded, 16)
            for r, (g, b) in enumerate((("ln1_g", "ln1_b"), ("ln2_g", "ln2_b"))):
                pool.dma_start(ln_g, t[g].to_broadcast([P, D])).then_inc(ln_rows_loaded[r], 16)
                pool.dma_start(ln_b, t[b].to_broadcast([P, D])).then_inc(ln_rows_loaded[r], 16)
                pool.wait_ge(ln_rows_loaded[r], 32)
                for n in range(NB):
                    pool.wait_ge(ln_gained[r], n + 1)
                    pool.tensor_tensor(y1[:, n, :], y1[:, n, :], ln_b, ALU.add).then_inc(ln_tile[r], 1)
                pool.wait_ge(ln_tile[r], NB)
                if r == 0:
                    split_weights(pool, "ffn1", w1_high, w1_low)
            pool.dma_start(x2_dram.rearrange("(b p) d -> p b d", p=P), y1).then_inc(x2_stored, 16)
            shift(pool, 0, hT, mod[:, 0:KT], "turn_h")
            for g in range(2):
                pool.iota(pool_inv[:, g, :], pattern=[[1, 16]], base=1, channel_multiplier=0,
                          allow_small_or_imprecise_dtypes=True).then_inc(counts_made, 1)
            do(pool.memset(selw[0:8, :, :], 1.0))
            pool.affine_select(out=selw[0:8, :, :], in_=selw[0:8, :, :], compare_op=ALU.is_equal, fill=0.0, base=0,
                               pattern=[[-1, 8], [0, P]], channel_multiplier=1).then_inc(selw_made, 1)
            pool.wait_ge(psum_free[0], L.pair_uses("turn_cum", 0, 0) + 1)
            for p in range(4):
                pool.wait_ge(psum_free[p], L.pair_uses("spread_cum", 0, p + 4) + 1)
            pool.wait_ge(br_bc_made, 4)
            for u, (h, b) in enumerate(heads8):
                N = P * (b + 1)
                if u >= 2:
                    pool.wait_ge(forget.logits_made, u - 1)
                pool.tensor_scalar(fbias[:, u % 2, 0:N], negcum[:, h, 0:N], cumq8[:, 8 * b + h:8 * b + h + 1], None,
                                   ALU.add).then_inc(fbias_made, 1)
                pool.wait_ge(fbias_made, 2 * u + 1)
                pool.tensor_tensor(fbias[:, u % 2, N - P:N], fbias[:, u % 2, N - P:N], causal8[:, :], ALU.add
                                   ).then_inc(fbias_made, 1)
            pool.wait_ge(forget.out_stored, len(heads8))
            pool.wait_ge(merged_step, 1 + 2 * KT)
            do(pool.memset(ones, 1.0))
            pool.sem_inc(ones_made, 1)
            pool.wait_ge(x2_stored, 16)
            pool.dma_start(x2_res, x2_dram.rearrange("(b p) d -> p b d", p=P)).then_inc(x2_back, 16)
            pool.wait_ge(x3_made, NB)
            pool.memset(y3, 0.0).then_inc(y3_zeroed, 1)
            for b in range(NB):
                pool.wait_ge(psum_free[L.pair("turn_h2", b)], L.pair_uses("turn_h2", 0, b) + 1)
                pool.tensor_tensor(shaped2[:, b % 2, :, :], shaped2[:, b % 2, :, :],
                                   mod[:, 3 * KT:4 * KT].unsqueeze(2).to_broadcast([P, KT, P]), ALU.add
                                   ).then_inc(h2_shifted, 1)
            split_weights(pool, "ffn2", w2_high, w2_low)

        @block.sync
        def _(sp):
            w1, w2 = t["w_in"][0], t["w_in_2"][0]

            def slot_free(stage, i, c):
                hold("sp", sp, weights_used[L.slot(stage, c)], L.slot_uses(stage, i, c))

            def load(stage, c, dst, src):
                sp.dma_start(dst, src).then_inc(weights_loaded[L.slot(stage, c)], 16)

            def feature_tiles(stage, w, column, width=P):
                rows = w.rearrange("(k p) n -> p k n", p=P)
                with loop(sp, L.iters[stage]) as i:
                    for c in range(len(L.slots[stage])):
                        slot_free(stage, i, c)
                        load(stage, c, ring[:, L.slot(stage, c), 0:KT * width].rearrange("p (k n) -> p k n", k=KT),
                             rows[:, :, bass.ds(column(i, c), width)])

            def token_tiles(stage, w, at=0):
                rows = w.rearrange("(k p) n -> p k n", p=P)
                with loop(sp, L.iters[stage]) as i:
                    for c in range(len(L.slots[stage])):
                        slot_free(stage, i, c)
                        load(stage, c, ring[:, L.slot(stage, c), :].rearrange("p (k n) -> p k n", k=2),
                             rows[:, 2 * c:2 * c + 2, bass.ds(i * 512 + at, 512)])

            def ffn_tiles(stage, tiles, w_up, w_down, column):
                rows_up = w_up.rearrange("(k p) n -> p k n", p=P)
                rows_down = w_down.rearrange("(i k p) n -> p i k n", p=P, k=2)
                with sp.Fori(0, L.iters[stage]) as i:
                    for c in range(tiles + 2):
                        slot_free(stage, i, c)
                        dst = ring[:, L.slot(stage, c), :]
                        if c < tiles:
                            load(stage, c, dst.rearrange("p (k n) -> p k n", k=KT),
                                 rows_up[:, :, bass.ds(column(i, c), P)])
                        else:
                            half = c - tiles
                            load(stage, c, dst.rearrange("p (a k n) -> p a k n", a=1, k=2),
                                 rows_down[:, bass.ds(i, 1), :, half * 512:(half + 1) * 512])

            for b in range(NB):
                sp.dma_start(x_tok[:, b, :], t["x"][0, tok(b), :]).then_inc(x_loaded[b], 16)
            feature_tiles("cqk", w1, lambda i, c: C_Q + c * P)
            rows = w1.rearrange("(k p) n -> p k n", p=P)
            for c in range(3):
                s = L.slot("idx", c)
                slot_free("idx", 0, c)
                dst = ring[:, s, :].rearrange("p (k n) -> p k n", k=KT)
                if c < 2:
                    load("idx", c, dst, rows[:, :, I_Q + c * P:I_Q + (c + 1) * P])
                else:
                    for r in range(4):
                        load("idx", c, dst[:, :, 32 * r:32 * r + 32], rows[:, :, I_K:I_K + 32])
            for c in range(4):
                slot_free("cv", 0, c)
                dst = ring[:, L.slot("cv", c), 0:528].rearrange("p (k n) -> p k n", k=2)
                load("cv", c, dst[:, :, 0:256], rows[:, 2 * c:2 * c + 2, C_V:C_V + 256])
                load("cv", c, dst[:, :, 256:264], rows[:, 2 * c:2 * c + 2, I_W:I_W + 8])
            token_tiles("auv", w1, A_U)
            feature_tiles("bqk", w1, lambda i, c: i * 512 + (B_Q + c * P))
            token_tiles("bv", w1, B_V)
            ada_rows = t["w_ada_2"][0].rearrange("(k p) n -> p k n", p=P)
            for j in range(N_ADA):
                slot_free("ada", 0, j)
                load("ada", j, ring[:, j % 4, :].rearrange("p (k n) -> p k n", k=KT), ada_rows[:, :, j * P:(j + 1) * P])
            token_tiles("out1", t["w_out"][0])
            ffn_tiles("ffn1", 4, t["w_gu"][0], t["w_down"][0], lambda i, c: i * 256 + ((c // 2) * P + (c % 2) * FH))
            feature_tiles("qk2", w2, lambda i, c: i * 512 + c * P)
            token_tiles("v2", w2, V2)
            feature_tiles("fl2", w2, lambda i, c: FL2, 8)
            feature_tiles("z2", w2, lambda i, c: i * 512 + (Z2 + c * P))
            gates = w2.rearrange("(k p) n -> p k n", p=P)
            branches = t["w_branch_2"][0].rearrange("(k p) n -> p k n", p=P)
            with sp.Fori(0, KT) as i:
                for c in range(4):
                    slot_free("branch", i, c)
                    src = branches[:, :, bass.ds(i * P, P)] if c == 3 else gates[:, :, bass.ds(i * P + (GL2 + c * D), P)]
                    load("branch", c, ring[:, c, :].rearrange("p (k n) -> p k n", k=KT), src)
            token_tiles("out2", t["w_out_2"][0])
            ffn_tiles("ffn2", 2, t["w_ff1_2"][0], t["w_ff2_2"][0], lambda i, c: i * 256 + c * P)
            for b in range(NB):
                sp.wait_ge(out_made, b + 1)
                sp.dma_start(out[0, tok(b), :], y3[:, b, :]).then_inc(out_stored, 16)
            sp.wait_ge(out_stored, 16 * NB)


_INS = ['x', 'w_in', 'gmlp_w_s', 'gmlp_b_s', 'gmlp_ln_g', 'gmlp_ln_b', 'lam_q1', 'lam_k1', 'lam_q2', 'lam_k2',
        'diff_subln_g', 'w_out', 'ln1_g', 'ln1_b', 'w_gu', 'w_down', 'ln2_g', 'ln2_b', 'c_2', 'w_ada_2', 'b_ada_2',
        'g_mix_pre_2', 'g_mix_post_2', 'g_ff_pre_2', 'g_ff_post_2', 'w_in_2', 'b_f_2', 'w_pool_2', 'pool_scale_2',
        'conv_w_2', 'w_branch_2', 'w_out_2', 'w_ff1_2', 'w_ff2_2']


def kernel(**inputs):
    import numpy as np
    import concourse.bacc as bacc
    from concourse.bass_utils import run_bass_kernel_spmd

    nc = bacc.Bacc("TRN2", target_bir_lowering=False, num_devices=1)
    arrays, handles = {}, {}
    for name in _INS:
        a = np.ascontiguousarray(inputs[name])
        arrays[f"in_{name}"] = a
        handles[name] = nc.dram_tensor(f"in_{name}", a.shape, mybir.dt.from_np(a.dtype), kind="ExternalInput").ap()
    result = nc.dram_tensor("result", (1, S, D), F32, kind="ExternalOutput").ap()
    program(nc, handles, result)
    return run_bass_kernel_spmd(nc, [arrays], core_ids=[0]).results[0]["result"]
```

```python
from contextlib import ExitStack, nullcontext

import concourse.bass as bass
from concourse import mybir

F32 = mybir.dt.float32
F32R = mybir.dt.float32r
BF16 = mybir.dt.bfloat16
ALU = mybir.AluOpType
ACT = mybir.ActivationFunctionType
AX = mybir.AxisListType

P = 128
S = 1024
D = 1024
NB = S // P
KT = D // P
FH = 2816
FT = FH // P
FF = 4096
FFT = FF // P
NEG = -8e30
ALPHA = 2.0 ** 0.25
EPS_LN = 1e-5
EPS_RMS = 1e-6
TOPK = 256
TAKEN = -3.3e38
FORBIDDEN = -1e37
LAM_INIT = 0.8 - 0.6
N_CONSTS = 17
SLOPES = [2.0 ** (-2.0 * (h + 1)) for h in range(4)]
POOL_WINDOWS = (2, 4, 8, 16)

A_U, B_Q, B_V, C_Q, C_V, I_Q, I_K, I_W = 0, 512, 1536, 2048, 2560, 2816, 3072, 3104
V2, FL2, Z2, GL2 = 1024, 1536, 1544, 2568
N_ADA = 6 * D // P

FOUR = [(0, 1), (1, 1), (2, 1), (3, 1)]
BY_FEATURE = [(0, 0), (1, 1), (2, 2), (3, 3)]
TURN = [(b % 4, None) for b in range(NB)]
SCORE_UNITS = [(b, h) for b in range(2, NB) for h in range(8)]


def by_token_units(chunks):
    return [(0, None), (1, None), (2, None), (3, chunks - 1)]


def by_token_half(pairs, chunk):
    return [(p, None) for p in pairs[:3]] + [(pairs[3], chunk)]


DOWN1_PAIRS = [(0, 1, 2, 3), (0, 1, 2, 3)]
DOWN2_PAIRS = [(2, 3, 0, 1), (0, 1, 2, 3)]

STAGES = [
    ("turn_x", 1, [], TURN),
    ("cqk", 1, FOUR, BY_FEATURE),
    ("idx", 1, [(0, 1), (1, 1), (2, 4)], BY_FEATURE[:3]),
    ("cv", 1, [(s, 2) for s in range(4)], by_token_units(4)),
    ("auv", 1, FOUR, by_token_units(4)),
    ("turn_ws", 1, [], [(0, None)]),
    ("score", 1, [], [(n % 4, None) for n in range(len(SCORE_UNITS))]),
    ("gmlp", 1, [], [(0, None), (1, None)]),
    ("bqk", 2, FOUR, BY_FEATURE),
    ("bv", 1, FOUR, by_token_units(4)),
    ("ada", 1, [(j % 4, 1) for j in range(N_ADA)], []),
    ("turn_mix", 1, [], TURN),
    ("out1", 2, FOUR, by_token_units(4)),
    ("turn_x1", 1, [], TURN),
    ("ffn1", FT // 2, FOUR + FOUR[:2],
     BY_FEATURE + by_token_half(DOWN1_PAIRS[0], 4) + by_token_half(DOWN1_PAIRS[1], 5)),
    ("turn_h", 1, [], TURN),
    ("qk2", 2, FOUR, BY_FEATURE),
    ("v2", 1, FOUR, by_token_units(4)),
    ("fl2", 1, [(0, 1)], [(0, 0)]),
    ("z2", 2, FOUR, BY_FEATURE),
    ("turn_cum", 1, [], [(0, None)]),
    ("spread_cum", 1, [], TURN),
    ("pool", 1, [], [(0, None), (1, None)]),
    ("branch", KT, FOUR, [(0, 0), (1, 1), (2, 2), (3, None), (0, None), (1, 3)]),
    ("rows", 1, [], [(2, None), (3, None)]),
    ("out2", 2, FOUR, by_token_units(4)),
    ("turn_h2", 1, [], TURN),
    ("ffn2", FFT // 2, FOUR,
     BY_FEATURE[:2] + by_token_half(DOWN2_PAIRS[0], 2) + by_token_half(DOWN2_PAIRS[1], 3)),
    ("end", 1, [], []),
]
SPLIT = {"out1": (4, 2), "ffn1": (6, 2), "qk2": (4, 2), "v2": (4, 2), "fl2": (1, 2), "z2": (4, 2),
         "branch": (3, 3), "out2": (4, 2), "ffn2": (4, 2)}


class Ledger:

    def __init__(self):
        self.iters, self.slots, self.units, self.base = {}, {}, {}, {}
        loads, uses, pairs, fulls = [0] * 4, [0] * 4, [0] * 4, [0] * 4
        parts, self.parts_base, self.high_base, highs = [1] * 3, {}, {}, 0
        for name, n, slots, units in STAGES:
            self.iters[name], self.slots[name], self.units[name] = n, slots, units
            self.base[name] = (list(loads), list(uses), list(pairs), list(fulls))
            for s, dmas in slots:
                loads[s] += n * dmas
                uses[s] += n
            self.parts_base[name], self.high_base[name] = list(parts), highs
            if name in SPLIT:
                chunks, slots_of_parts = SPLIT[name]
                assert n == 1 or chunks % slots_of_parts == 0
                highs += n * chunks
                for c in range(chunks):
                    parts[c % slots_of_parts] += n
            for p, chunk in units:
                pairs[p] += n
                fulls[p] += n * (chunk is None)

    def slot(self, stage, c):
        return self.slots[stage][c][0]

    def pair(self, stage, u):
        return self.units[stage][u][0]

    def loaded(self, stage, i, c):
        mine = self.slot(stage, c)
        dmas = [(s == mine) * d for s, d in self.slots[stage]]
        return (self.base[stage][0][mine] + sum(dmas[:c + 1])) * 16 + i * (sum(dmas) * 16)

    def slot_uses(self, stage, i, c):
        mine = self.slot(stage, c)
        used = [s == mine for s, _ in self.slots[stage]]
        return self.base[stage][1][mine] + sum(used[:c]) + i * sum(used)

    def pair_uses(self, stage, i, u):
        mine = self.pair(stage, u)
        used = [p == mine for p, _ in self.units[stage]]
        return self.base[stage][2][mine] + sum(used[:u]) + i * sum(used)

    def parts_uses(self, stage, i, c):
        chunks, slots = SPLIT[stage]
        return self.parts_base[stage][c % slots] + c // slots + i * (chunks // slots)

    def is_split(self, stage, c):
        return stage in SPLIT and c < SPLIT[stage][0]

    def parts_slot(self, stage, c):
        return c % SPLIT[stage][1]

    def full(self, stage, i, u):
        mine, chunk = self.units[stage][u]
        if chunk is not None and self.is_split(stage, chunk):
            return "parts_used", self.parts_slot(stage, chunk), self.parts_uses(stage, i, chunk) + 1
        if chunk is not None:
            return "weights_used", self.slot(stage, chunk), self.slot_uses(stage, i, chunk) + 1
        used = [p == mine and c is None for p, c in self.units[stage]]
        return "psum_full", mine, self.base[stage][3][mine] + sum(used[:u + 1]) + i * sum(used)


def loop(eng, n):
    return nullcontext(0) if n == 1 else eng.Fori(0, n)


def program(nc, t, out):
    L = Ledger()
    with ExitStack() as ctx:
        def sem(name):
            return ctx.enter_context(nc.semaphore(name))

        KB = 256
        END = 186 * KB
        arena = ctx.enter_context(nc.sbuf_tensor("arena", [P, END], F32))
        arena_base = nc.sbuf_base - END * 4

        def view(kb, *dims):
            n = 1
            for d in dims:
                n *= d
            a = arena[:, int(kb * KB):int(kb * KB) + n]
            names = "abcd"[:len(dims)]
            if len(dims) > 1:
                a = a.rearrange(f"p ({' '.join(names)}) -> p {' '.join(names)}",
                                **{x: d for x, d in zip(names[1:], dims[1:])})
            return a

        def rounded(name, kb, *dims):
            return nc.alloc_sbuf_tensor_at(name, [P, *dims], F32R, offset=arena_base + kb * 1024)

        def small(name, *shape):
            return ctx.enter_context(nc.sbuf_tensor(name, list(shape), F32))

        xT = view(0, KT, S)
        mix = view(0, NB, D - 256)
        y1 = view(0, NB, D)
        x_tok = view(32, NB, D)
        bqkT = view(32, 8, S)
        mixT_high, mixT_low = rounded("mixT_high", 32, KT, S), rounded("mixT_low", 120, KT, S)
        wo1_high, wo1_low = rounded("wo1_high", 168, 2, 1024), rounded("wo1_low", 176, 2, 1024)
        x1T_high, x1T_low = rounded("x1T_high", 32, KT, S), rounded("x1T_low", 64, KT, S)
        cqkT = view(64, 4, S)
        x_res = view(88, NB, D)
        au = view(80, NB, 256)
        av = view(88, NB, 256)
        mask_at = {b: sum(P * (c + 1) for c in range(2, b)) for b in range(2, NB)}
        mask_all = view(88, 2112).bitcast(BF16)
        mask = {b: mask_all[:, mask_at[b]:mask_at[b] + P * (b + 1)] for b in range(2, NB)}
        score_off = {b: int(141.5 * KB) + sum(P * (c + 1) for c in range(2, b)) for b in range(2, NB)}
        score = {b: arena[:, score_off[b]:score_off[b] + P * (b + 1)] for b in range(2, NB)}
        bv = view(97, NB, 512)
        cvw = view(113, NB, 264)
        iqT = view(121.5, 2, S)
        ikT = view(129.5, S)
        cbias = view(141.5, 2, S)
        logit = view(24, 2, S)
        relu = view(133.5, 2, S)
        prob = view(121.5, 4, S)
        probT = view(158, 2, NB, P)
        ws_tok = view(159, 4, P)
        v_sq = view(141.5, NB * 4, 64)
        dist = view(165.5, S)
        bias8 = view(169.5, 4, S)
        hid1_high, hid1_low = rounded("hid1_high", 96, 2, S), rounded("hid1_low", 104, 2, S)
        w1_high, w1_low = rounded("w1_high", 112, 2, 1024), rounded("w1_low", 120, 2, 1024)
        silu_t = view(152, 2, S)
        ln_g, ln_b = view(160, D), view(164, D)
        o_sq = view(24, 16, P)
        hT_high, hT_low = rounded("hT_high", 32, KT, S), rounded("hT_low", 148, KT, S)
        hT_low_back = rounded("hT_low_back", 0, KT, S)
        shaped = nc.alloc_sbuf_tensor_at("shaped", [P, 2, KT, P], F32, offset=arena_base + 72 * 1024)
        win2_high, win2_low = rounded("win2_high", 0, 2, 1024), rounded("win2_low", 8, 2, 1024)
        wbr_high, wbr_low = rounded("wbr_high", 116, 3, 1024), rounded("wbr_low", 128, 3, 1024)
        xhat = view(64, 2, D)
        qk2T = view(64, 8, S)
        z2T = view(96, 8, S)
        v2 = view(128, NB, 512)
        fl = view(144, S)
        brT = view(148, KT, S)
        pad_a = view(148, 16 + S)
        pad_b = view(152.25, 16 + S)
        ps_t = view(156.5, S)
        lsf_a = view(16, S)
        lsf_b = view(20, S)
        negcum = view(0, 8, S)
        logit2 = view(96, 2, S)
        prob2 = view(104, 2, S)
        probT2 = view(112, 2, NB, P)
        fbias = view(120, 2, S)
        sig = view(96, 3, S)
        mg = view(108, 2, S)
        mergedT = nc.alloc_sbuf_tensor_at("mergedT", [P, KT, S], F32, offset=arena_base + 64 * 1024)
        mergedT_high, mergedT_low = rounded("mergedT_high", 0, KT, S), rounded("mergedT_low", 32, KT, S)
        wo2_high, wo2_low = rounded("wo2_high", 144, 2, 1024), rounded("wo2_low", 152, 2, 1024)
        y2 = view(96, NB, D)
        x2_res = view(128, NB, D)
        row_gain = view(160, D)
        diag = view(164, D)
        xhat2 = view(168, 2, D)
        h2T_high, h2T_low = rounded("h2T_high", 0, KT, S), rounded("h2T_low", 32, KT, S)
        shaped2 = nc.alloc_sbuf_tensor_at("shaped2", [P, 2, KT, P], F32, offset=arena_base + 128 * 1024)
        hid2_high, hid2_low = rounded("hid2_high", 128, 2, S), rounded("hid2_low", 136, 2, S)
        w2_high, w2_low = rounded("w2_high", 144, 2, 1024), rounded("w2_low", 152, 2, 1024)
        relu_t = view(160, 2, S)
        y3 = view(64, NB, D)
        row_gain2, diag2 = view(180, D), view(176, D)
        junks = [view(148, S), view(176, S), view(176, S), view(56, S)]

        ring = small("ring", P, 4, 1024)
        ident = small("ident", P, P)
        causal8 = small("causal8", P, P)
        wsT = small("wsT", P, 4, P)
        pool_w = small("pool_w", P, 2, P)
        misc = small("misc", P, 440)
        at = [0]

        def cut(n, *dims):
            a = misc[:, at[0]:at[0] + n]
            at[0] += n
            return a

        c_col, c_act, b_ada, mod = cut(KT), cut(KT), cut(N_ADA), cut(N_ADA)
        g_mix_pre, g_ff_pre, g_mix_post, g_ff_post = cut(KT), cut(KT), cut(KT), cut(KT)
        gain_m, gain_f, gate_m, gate_f = cut(KT), cut(KT), cut(KT), cut(KT)
        pscale, conv_w, b_f = cut(2), cut(6), cut(1)
        bs_col = cut(4)
        expsum, rowmin, rcp, coef = cut(8), cut(8), cut(8), cut(8)
        top8 = cut(48)
        lam_s, lam_e, neglam = cut(2), cut(2), cut(1)
        stats = cut(NB * 2)
        bn = cut(12)
        rstd, nmr, ssq = cut(NB), cut(NB), cut(NB)
        cumq8 = cut(64)
        o_ssq = cut(32)
        pool_inv = view(184, 2, 16)
        lam_v = view(163.75, 4, 64)
        vstat_lam = view(165, 2, 64)
        vstat = view(163.25, 3, 32)
        aln = view(161, 2, 256)
        subln = view(185.5, P)
        ones = view(185, P)
        selw = view(180, 8, P)

        PS = ctx.enter_context(nc.psum_tensor("PS", [P, 8, 512], F32))

        def pair(p):
            return PS[:, 2 * p:2 * p + 2, :]

        def flat(p):
            return pair(p).rearrange("p b n -> p (b n)")

        h_low_dram = nc.dram_tensor("h_low_spill", [P, KT, S], F32R).ap()
        x2_dram = nc.dram_tensor("x2_spill", [S, D], F32).ap()

        weights_loaded = [sem(f"weights_loaded{s}") for s in range(4)]
        weights_used = [sem(f"weights_used{s}") for s in range(4)]
        parts_used = [sem(f"parts_used{q}") for q in range(3)]
        weights_high = sem("weights_high")
        psum_full = [sem(f"psum_full{p}") for p in range(4)]
        psum_free = [sem(f"psum_free{p}") for p in range(4)]
        tick = {e: sem(f"tick_{e}") for e in ("pe", "act", "dve", "pool", "sp")}
        dve_chain = sem("dve_chain")
        act_chain = sem("act_chain")
        pool_chain = sem("pool_chain")
        x_loaded = [sem(f"x_loaded{b}") for b in range(NB)]
        consts_loaded = sem("consts_loaded")
        ws_loaded, ws_masked = sem("ws_loaded"), sem("ws_masked")
        ident_made = sem("ident_made")
        dist_made = sem("dist_made")
        bias_made = sem("bias_made")
        lam_sums = sem("lam_sums")
        lam_exps = sem("lam_exps")
        c_act_made = sem("c_act_made")
        mod_made = sem("mod_made")
        ada_done = sem("ada_done")
        v_normed = sem("v_normed")
        gmlp_var = sem("gmlp_var")
        gmlp_sqrt = sem("gmlp_sqrt")
        score_added = sem("score_added")
        topk_done = sem("topk_done")
        cbias_made = sem("cbias_made")
        fbias_made = sem("fbias_made")
        o_var = sem("o_var")
        o_sqrt = sem("o_sqrt")
        mix_done = sem("mix_done")
        xres_loaded = sem("xres_loaded")
        ln_rows_loaded = [sem("ln1_rows_loaded"), sem("ln2_rows_loaded")]
        ln_var = [sem("ln1_var"), sem("ln2_var")]
        ln_sqrt = [sem("ln1_sqrt"), sem("ln2_sqrt")]
        ln_scaled = [sem("ln1_scaled"), sem("ln2_scaled")]
        ln_tile = [sem("ln1_tile"), sem("ln2_tile")]
        hid_high, hid_made = ([sem(f"{n}{r}") for r in (1, 2)] for n in ("hid_high", "hid_made"))
        hid_squared = sem("hid_squared")
        y1_grown, y3_zeroed = sem("y1_grown"), sem("y3_zeroed")
        mix_high_made, x1_high_made = sem("mix_high_made"), sem("x1_high_made")
        h_high_made, h_shifted = ([sem(f"{n}{r}") for r in (1, 2)] for n in ("h_high_made", "h_shifted"))
        h_low_stored, h_low_back = sem("h_low_stored"), sem("h_low_back")
        merged_high_made, merged_split = sem("merged_high_made"), sem("merged_split")
        rms_sum = [sem(f"rms_sum{r}") for r in range(4)]
        rms_var = [sem(f"rms_var{r}") for r in range(4)]
        rms_sqrt = [sem(f"rms_sqrt{r}") for r in range(4)]
        rms_rstd = [sem(f"rms_rstd{r}") for r in range(4)]
        x2_stored, x2_back = sem("x2_stored"), sem("x2_back")
        xhat_made = [sem("xhat_made"), sem("xhat2_made")]
        h_made = [sem("h_made"), sem("h2_made")]
        fl_exp, fl_ln, cum_done = sem("fl_exp"), sem("fl_ln"), sem("cum_done")
        selw_made = sem("selw_made")
        pool_w_loaded, pool_w_zeroed = sem("pool_w_loaded"), sem("pool_w_zeroed")
        pooled = sem("pooled")
        br_bc_made = sem("br_bc_made")
        merged_step = sem("merged_step")
        topk_step = sem("topk_step")
        ones_made, counts_made = sem("ones_made"), sem("counts_made")
        ln_gained = [sem("ln1_gained"), sem("ln2_gained")]
        diag_made = sem("diag_made")
        y2_scaled, x3_made = sem("y2_scaled"), sem("x3_made")
        y3_scaled, out_made, out_stored = sem("y3_scaled"), sem("out_made"), sem("out_stored")

        def hold(name, eng, s, value):
            if isinstance(value, int):
                if value > 0:
                    eng.wait_ge(s, value)
            else:
                eng.wait_ge(s, value)
                eng.sem_inc(tick[name], 1)

        class Attention:
            def __init__(self, name, maps, units, q, k, v, dv, bias, dest, bufs, transposed, ada_from):
                self.name, self.maps, self.units = name, maps, units
                self.q, self.k, self.v, self.dv, self.bias, self.dest = q, k, v, dv, bias, dest
                self.logit, self.prob, self.probT = bufs
                self.n_prob = self.prob.shape[1]
                self.transposed, self.ada_from = transposed, ada_from
                self.out_banks = 2 if ada_from is None else 1
                self.scores_done = sem(name + "_scores_done")
                self.logits_made = sem(name + "_logits_made")
                self.probs_made = sem(name + "_probs_made")
                self.probs_ready = sem(name + "_probs_ready")
                self.turned = sem(name + "_turned")
                self.probsT_made = sem(name + "_probsT_made")
                self.out_done = sem(name + "_out_done")
                self.out_stored = sem(name + "_out_stored")

            def slot(self, u, m):
                return (u * self.maps + m) % self.n_prob

            def pe(self, pe):
                def scores(u):
                    h, b = self.units[u]
                    for m in range(self.maps):
                        n = u * self.maps + m
                        if n >= 2:
                            pe.wait_ge(self.logits_made, n - 1)
                        for c in range(0, P * (b + 1), 512):
                            w = min(512, P * (b + 1) - c)
                            mm = pe.matmul(PS[:, 2 * (n % 2) + c // 512, 0:w], self.q(h, m, b),
                                           self.k(h, m, c, w), start=True, stop=True)
                        mm.then_inc(self.scores_done, 1)

                def turn(u):
                    _, b = self.units[u]
                    pe.wait_ge(self.probs_ready, u + 1)
                    if u >= 1:
                        pe.wait_ge(self.probsT_made, u)
                    for s in range(b + 1):
                        mm = pe.transpose(PS[:, 4 + s // 4, (s % 4) * P:(s % 4 + 1) * P],
                                          self.prob[:, self.slot(u, 0), s * P:(s + 1) * P], ident[:, :])
                    mm.then_inc(self.turned, 1)

                def times_v(u):
                    h, b = self.units[u]
                    pe.wait_ge(self.probsT_made, u + 1)
                    if u >= self.out_banks:
                        pe.wait_ge(self.out_stored, u - self.out_banks + 1)
                    for s in range(b + 1):
                        pT = self.probT[:, u % 2, s, :]
                        if self.transposed:
                            lo = 64 * (h % 2)
                            mm = pe.matmul(PS[lo:lo + self.dv, 6 + u % self.out_banks, 0:P],
                                           self.v(h, s), pT, start=(s == 0), stop=(s == b))
                        else:
                            mm = pe.matmul(PS[:, 6 + u % self.out_banks, 0:self.dv],
                                           pT, self.v(h, s), start=(s == 0), stop=(s == b))
                    mm.then_inc(self.out_done, 1)

                scores(0)
                for u in range(len(self.units)):
                    if u + 1 < len(self.units):
                        scores(u + 1)
                    if self.ada_from is not None and self.ada_from + u < N_ADA:
                        ada(pe, self.ada_from + u)
                    if u >= 1:
                        times_v(u - 1)
                    turn(u)
                times_v(len(self.units) - 1)

            def act(self, act):
                def exps(u):
                    _, b = self.units[u]
                    N = P * (b + 1)
                    for m in range(self.maps):
                        n = u * self.maps + m
                        act.wait_ge(self.logits_made, n + 1)
                        back = self.n_prob // self.maps
                        if u >= back:
                            act.wait_ge(self.turned, u - back + 1)
                        act.activation(self.prob[:, self.slot(u, m), 0:N], self.logit[:, n % 2, 0:N],
                                       ACT.Exp, bias=rowmin[:, n % 8:n % 8 + 1], scale=-1.0,
                                       accum_out=expsum[:, n % 8:n % 8 + 1]).then_inc(self.probs_made, 1)

                def copy_turned(u):
                    _, b = self.units[u]
                    act.wait_ge(self.turned, u + 1)
                    if u >= 2:
                        act.wait_ge(self.out_done, u - 1)
                    act.copy(self.probT[:, u % 2, 0:b + 1, :].rearrange("p s n -> p (s n)"),
                             flat(2)[:, 0:P * (b + 1)]).then_inc(self.probsT_made, 1)

                exps(0)
                for u in range(len(self.units)):
                    if u + 1 < len(self.units):
                        exps(u + 1)
                    copy_turned(u)

            def dve(self, dve, link, beside=None):
                def logits(u):
                    h, b = self.units[u]
                    N = P * (b + 1)
                    for m in range(self.maps):
                        n = u * self.maps + m
                        dve.wait_ge(self.scores_done, n + 1)
                        if n >= 2:
                            dve.wait_ge(self.probs_made, n - 1)
                        if self.bias is not None:
                            bias, s, value = self.bias(u)
                            if s is not None:
                                dve.wait_ge(s, value)
                        dve.tensor_tensor_reduce(out=self.logit[:, n % 2, 0:N],
                                                 in0=flat(n % 2)[:, 0:N], in1=bias, scale=-0.125,
                                                 scalar=3e38, op0=ALU.add, op1=ALU.min,
                                                 accum_out=rowmin[:, n % 8:n % 8 + 1]).then_inc(self.logits_made, 1)

                def combine(u):
                    _, b = self.units[u]
                    N = P * (b + 1)
                    n = u * self.maps
                    dve.wait_ge(self.probs_made, n + self.maps)
                    r = rcp[:, n % 8:n % 8 + 1]
                    if self.maps == 2:
                        dve.reciprocal(rcp[:, n % 8:n % 8 + 2], expsum[:, n % 8:n % 8 + 2]).then_inc(dve_chain, 1)
                        link()
                        dve.scalar_tensor_tensor(out=coef[:, n % 8:n % 8 + 1], in0=expsum[:, n % 8:n % 8 + 1],
                                                 scalar=neglam[:, 0:1], in1=rcp[:, n % 8 + 1:n % 8 + 2],
                                                 op0=ALU.mult, op1=ALU.mult).then_inc(dve_chain, 1)
                        link()
                        p0, p1 = (self.prob[:, self.slot(u, m), 0:N] for m in range(2))
                        dve.scalar_tensor_tensor(out=p0, in0=p1, scalar=coef[:, n % 8:n % 8 + 1], in1=p0,
                                                 op0=ALU.mult, op1=ALU.add).then_inc(self.probs_ready, 1)
                    elif self.transposed:
                        dve.reciprocal(r, expsum[:, n % 8:n % 8 + 1]).then_inc(dve_chain, 1)
                        link()
                        p0 = self.prob[:, self.slot(u, 0), 0:N]
                        dve.tensor_scalar(p0, p0, r, None, ALU.mult).then_inc(self.probs_ready, 1)
                    else:
                        dve.reciprocal(r, expsum[:, n % 8:n % 8 + 1]).then_inc(self.probs_ready, 1)

                def store(u):
                    h, b = self.units[u]
                    n = u * self.maps
                    dve.wait_ge(self.out_done, u + 1)
                    lo = 64 * (h % 2)
                    if self.transposed:
                        dve.tensor_copy(self.dest(h, b), PS[lo:lo + self.dv, 6 + u % self.out_banks, 0:P]
                                        ).then_inc(self.out_stored, 1)
                    else:
                        if self.maps == 1:
                            dve.wait_ge(self.probs_ready, u + 1)
                        dve.tensor_scalar(self.dest(h, b), PS[:, 6 + u % self.out_banks, 0:self.dv],
                                          rcp[:, n % 8:n % 8 + 1], None, ALU.mult).then_inc(self.out_stored, 1)

                logits(0)
                for u in range(len(self.units)):
                    if u + 1 < len(self.units):
                        logits(u + 1)
                    combine(u)
                    if u >= 1:
                        store(u - 1)
                    if beside is not None:
                        beside(u)
                store(len(self.units) - 1)
                dve.wait_ge(self.out_stored, len(self.units))

        heads4 = [(h, b) for h in range(4) for b in range(NB)]
        heads8 = [(h, b) for h in range(8) for b in range(NB)]

        def tok(b):
            return slice(b * P, (b + 1) * P)

        def b_bias(u):
            h, b = heads4[u]
            return bias8[:, h, P * (NB - 1 - b):S], bias_made, 4

        def c_bias(u):
            h, b = heads4[u]
            if b < 2:
                return bias8[:, h, P * (NB - 1 - b):S], None, 0
            k = h * (NB - 2) + b - 2
            return cbias[:, k % 2, 0:P * (b + 1)], cbias_made, k + 1

        def f_bias(u):
            return fbias[:, u % 2, 0:P * (heads8[u][1] + 1)], fbias_made, 2 * (u + 1)

        diff = Attention(
            "diff", 2, heads4,
            lambda h, m, b: bqkT[64 * m:64 * m + 64, h, tok(b)],
            lambda h, m, c, w: bqkT[64 * m:64 * m + 64, 4 + h, c:c + w],
            lambda h, s: bv[:, s, h * P:(h + 1) * P], P, b_bias,
            lambda h, b: mix[:, b, h * P:(h + 1) * P],
            (logit, prob, probT), False, 0)
        sparse = Attention(
            "sparse", 1, heads4,
            lambda h, m, b: cqkT[64 * (h % 2):64 * (h % 2) + 64, h // 2, tok(b)],
            lambda h, m, c, w: cqkT[64 * (h % 2):64 * (h % 2) + 64, 2 + h // 2, c:c + w],
            lambda h, s: cvw[:, s, h * 64:(h + 1) * 64], 64, c_bias,
            lambda h, b: mix[:, b, 512 + h * 64:512 + (h + 1) * 64],
            (logit, prob, probT), False, 32)
        forget = Attention(
            "forget", 1, heads8,
            lambda h, m, b: qk2T[64 * (h % 2):64 * (h % 2) + 64, h // 2, tok(b)],
            lambda h, m, c, w: qk2T[64 * (h % 2):64 * (h % 2) + 64, 4 + h // 2, c:c + w],
            lambda h, s: v2[:, s, h * 64:(h + 1) * 64], 64, f_bias,
            lambda h, b: brT[64 * (h % 2):64 * (h % 2) + 64, h // 2, tok(b)],
            (logit2, prob2, probT2), True, None)

        def weights_here(pe, stage, i, c):
            hold("pe", pe, weights_loaded[L.slot(stage, c)], L.loaded(stage, i, c))

        def pair_here(pe, stage, i, u):
            hold("pe", pe, psum_free[L.pair(stage, u)], L.pair_uses(stage, i, u))

        def ada(pe, j):
            weights_here(pe, "ada", 0, j)
            w = ring[:, j % 4, :].rearrange("p (k n) -> p k n", k=KT)
            if j == 0:
                pe.wait_ge(c_act_made, 1)
            for k in range(KT):
                mm = pe.matmul(PS[:, 7, j:j + 1], w[:, k, :], c_act[:, k:k + 1], start=(k == 0), stop=(k == KT - 1))
            mm.then_inc(weights_used[j % 4], 1)

        def split_here(pe, stage, i, c):
            hold("pe", pe, weights_used[L.slot(stage, c)], L.slot_uses(stage, i, c) + 1)

        def split_unit(pe, stage, i, c, x_high, x_low, w_parts):
            p, q = L.pair(stage, c), L.parts_slot(stage, c)
            w_high, w_low = w_parts
            split_here(pe, stage, i, c)
            pair_here(pe, stage, i, c)
            for half in range(2):
                for k in range(KT):
                    for n, (w, x) in enumerate(((w_high, x_high), (w_high, x_low), (w_low, x_high))):
                        mm = pe.matmul(PS[:, 2 * p + half, :], w[:, q, k * P:(k + 1) * P],
                                       x[:, k, half * 512:(half + 1) * 512],
                                       start=(k == 0 and n == 0), stop=(k == KT - 1 and n == 2))
            mm.then_inc(parts_used[q], 1)

        def by_feature_split(pe, stage, x_high, x_low, w_parts):
            with loop(pe, L.iters[stage]) as i:
                for c in range(len(L.slots[stage])):
                    split_unit(pe, stage, i, c, x_high, x_low, w_parts)

        def by_token_split(pe, stage, x_high, x_low, w_parts, tile_here=lambda i, k: None):
            n_chunks = len(L.slots[stage])
            w_high, w_low = w_parts
            with loop(pe, L.iters[stage]) as i:
                for c in range(n_chunks):
                    q = L.parts_slot(stage, c)
                    split_here(pe, stage, i, c)
                    for kk in range(2):
                        k = 2 * c + kk
                        tile_here(i, k)
                        for b in range(NB):
                            if k == 0 and b % 2 == 0:
                                pair_here(pe, stage, i, b // 2)
                            for n, (x, w) in enumerate(((x_high, w_high), (x_high, w_low), (x_low, w_high))):
                                mm = pe.matmul(PS[:, b, :], x[:, k, tok(b)], w[:, q, kk * 512:(kk + 1) * 512],
                                               start=(k == 0 and n == 0), stop=(k == 2 * n_chunks - 1 and n == 2))
                            if k == 2 * n_chunks - 1 and b % 2 == 1 and b < NB - 1:
                                mm.then_inc(psum_full[b // 2], 1)
                    mm.then_inc(parts_used[q], 1)

        def by_feature(pe, stage, source, width=P):
            with loop(pe, L.iters[stage]) as i:
                for c in range(len(L.slots[stage])):
                    s, p = L.slot(stage, c), L.pair(stage, c)
                    w = ring[:, s, 0:KT * width].rearrange("p (k n) -> p k n", k=KT)
                    weights_here(pe, stage, i, c)
                    pair_here(pe, stage, i, c)
                    for half in range(2):
                        for k in range(KT):
                            mm = pe.matmul(PS[0:width, 2 * p + half, :], w[:, k, :],
                                           source[:, k, half * 512:(half + 1) * 512],
                                           start=(k == 0), stop=(k == KT - 1))
                    mm.then_inc(weights_used[s], 1)

        def by_token(pe, stage, source, width=512):
            n = len(L.slots[stage])
            with loop(pe, L.iters[stage]) as i:
                for c in range(n):
                    s = L.slot(stage, c)
                    weights_here(pe, stage, i, c)
                    for kk in range(2):
                        k = 2 * c + kk
                        for b in range(NB):
                            if k == 0 and b % 2 == 0:
                                pair_here(pe, stage, i, b // 2)
                            last = k == 2 * n - 1 and b % 2 == 1
                            mm = pe.matmul(PS[:, b, 0:width], source[:, k, tok(b)],
                                           ring[:, s, kk * width:(kk + 1) * width],
                                           start=(k == 0), stop=(k == 2 * n - 1))
                            if last and b < NB - 1:
                                mm.then_inc(psum_full[b // 2], 1)
                    mm.then_inc(weights_used[s], 1)

        def ffn(pe, r, stage, tiles, x_high, x_low, hid_parts, w_parts, down_pairs):
            w_high, w_low = w_parts
            hid_hi, hid_lo = hid_parts
            with pe.Fori(0, L.iters[stage]) as i:
                for c in range(tiles):
                    split_unit(pe, stage, i, c, x_high, x_low, w_parts)
                for half in range(2):
                    c = tiles + half
                    split_here(pe, stage, i, c)
                    for k in range(2):
                        if half == 0:
                            hold("pe", pe, hid_made[r], 2 * i + (3 + k))
                        for at, p in enumerate(down_pairs[half]):
                            if k == 0:
                                pair_here(pe, stage, i, tiles + 4 * half + at)
                            for b in (2 * p, 2 * p + 1):
                                for n, (h, w) in enumerate(((hid_hi, w_high), (hid_hi, w_low), (hid_lo, w_high))):
                                    mm = pe.matmul(PS[:, b, :], h[:, k, tok(b)], w[:, c % 2, k * 512:(k + 1) * 512],
                                                   start=(k == 0 and n == 0), stop=(k == 1 and n == 2))
                            if k == 1:
                                mm.then_inc(psum_full[p] if at < 3 else parts_used[c % 2], 1)

        def turn(pe, stage, source, ready):
            for b in range(NB):
                p = L.pair(stage, b)
                ready(b)
                pair_here(pe, stage, 0, b)
                for k in range(KT):
                    mm = pe.transpose(PS[:, 2 * p + k // 4, (k % 4) * P:(k % 4 + 1) * P],
                                      source(b, k), ident[:, :])
                mm.then_inc(psum_full[p], 1)

        def all_pairs_free(eng, stage):
            for p in range(4):
                eng.wait_ge(psum_free[p], L.base[stage][2][p])

        block = ctx.enter_context(nc.Block())

        @block.tensor
        def _(pe):
            for used in parts_used:
                pe.sem_inc(used, 1)
            pe.wait_ge(ident_made, 2)
            turn(pe, "turn_x", lambda b, k: x_tok[:, b, k * P:(k + 1) * P], lambda b: pe.wait_ge(x_loaded[b], 16))
            all_pairs_free(pe, "cqk")
            by_feature(pe, "cqk", xT)
            by_feature(pe, "idx", xT)
            by_token(pe, "cv", xT, 264)
            by_token(pe, "auv", xT)
            pe.wait_ge(ws_masked, 1)
            pair_here(pe, "turn_ws", 0, 0)
            for g in range(4):
                mm = pe.transpose(PS[:, 0, g * P:(g + 1) * P], ws_tok[:, g, :], ident[:, :])
            mm.then_inc(psum_full[0], 1)
            pe.wait_ge(psum_free[0], L.pair_uses("idx", 0, 0) + 1)
            pe.wait_ge(psum_free[1], L.pair_uses("idx", 0, 1) + 1)
            pe.wait_ge(psum_free[2], L.pair_uses("idx", 0, 2) + 1)
            for n, (b, h) in enumerate(SCORE_UNITS):
                p = L.pair("score", n)
                lo = 32 * (h % 4)
                pair_here(pe, "score", 0, n)
                for c in range(0, P * (b + 1), 512):
                    w = min(512, P * (b + 1) - c)
                    mm = pe.matmul(PS[:, 2 * p + c // 512, 0:w], iqT[lo:lo + 32, h // 4, tok(b)],
                                   ikT[lo:lo + 32, c:c + w], start=True, stop=True)
                mm.then_inc(psum_full[p], 1)
            pe.wait_ge(v_normed, 1)
            for g in range(4):
                if g % 2 == 0:
                    pair_here(pe, "gmlp", 0, g // 2)
                mm = pe.matmul(PS[:, g, :], wsT[:, g, :], av[:, :, g * 64:(g + 1) * 64],
                               start=True, stop=True)
                if g % 2 == 1:
                    mm.then_inc(psum_full[g // 2], 1)
            by_feature(pe, "bqk", xT)
            by_token(pe, "bv", xT)
            all_pairs_free(pe, "ada")
            diff.pe(pe)
            sparse.pe(pe)
            hold("pe", pe, sparse.out_done, len(heads4))
            pe.sem_inc(ada_done, 1)
            turn(pe, "turn_mix",
                 lambda b, k: au[:, b, k * P:(k + 1) * P] if k < 2 else mix[:, b, (k - 2) * P:(k - 1) * P],
                 lambda b: pe.wait_ge(mix_done, 1))
            all_pairs_free(pe, "out1")
            by_token_split(pe, "out1", mixT_high, mixT_low, (wo1_high, wo1_low))
            turn(pe, "turn_x1", lambda b, k: y1[:, b, k * P:(k + 1) * P], lambda b: pe.wait_ge(ln_tile[0], b + 1))
            all_pairs_free(pe, "ffn1")
            ffn(pe, 0, "ffn1", 4, x1T_high, x1T_low, (hid1_high, hid1_low), (w1_high, w1_low), DOWN1_PAIRS)
            turn(pe, "turn_h", lambda b, k: xhat[:, b % 2, k * P:(k + 1) * P],
                 lambda b: pe.wait_ge(xhat_made[0], b + 1))
            pe.wait_ge(h_made[0], NB)
            by_feature_split(pe, "qk2", hT_high, hT_low, (win2_high, win2_low))
            by_token_split(pe, "v2", hT_high, hT_low, (win2_high, win2_low))
            by_feature_split(pe, "fl2", hT_high, hT_low, (win2_high, win2_low))
            by_feature_split(pe, "z2", hT_high, hT_low, (win2_high, win2_low))
            pe.wait_ge(cum_done, 1)
            pair_here(pe, "turn_cum", 0, 0)
            for b in range(NB):
                mm = pe.transpose(PS[:, 0, b * 8:b * 8 + 8], fl[0:8, tok(b)], ident[0:8, 0:8])
            mm.then_inc(psum_full[0], 1)
            pe.wait_ge(selw_made, 1)
            for h in range(8):
                p = L.pair("spread_cum", h)
                pair_here(pe, "spread_cum", 0, h)
                for half in range(2):
                    mm = pe.matmul(PS[:, 2 * p + half, :], selw[0:8, h, :], fl[0:8, half * 512:(half + 1) * 512],
                                   start=True, stop=True)
                mm.then_inc(psum_full[p], 1)
            pe.wait_ge(pool_w_loaded, 64)
            for g in range(2):
                pe.wait_ge(pooled, g + 1)
                pair_here(pe, "pool", 0, g)
                for half in range(2):
                    mm = pe.matmul(PS[:, 2 * g + half, :], pool_w[:, g, :], z2T[:, g, half * 512:(half + 1) * 512],
                                   start=True, stop=True)
                mm.then_inc(psum_full[g], 1)
            all_pairs_free(pe, "branch")
            forget.pe(pe)
            pe.wait_ge(forget.out_stored, len(heads8))
            pe.wait_ge(br_bc_made, 4)
            pe.wait_ge(h_low_back, 16 * KT)
            with loop(pe, KT) as i:
                for c in range(3):
                    split_unit(pe, "branch", i, c, hT_high, hT_low_back, (wbr_high, wbr_low))
                weights_here(pe, "branch", i, 3)
                w = ring[:, 3, :].rearrange("p (k n) -> p k n", k=KT)
                for br, ks in enumerate((range(0, 4), range(4, 6), range(6, 8))):
                    p = L.pair("branch", 3 + br)
                    pair_here(pe, "branch", i, 3 + br)
                    for half in range(2):
                        for k in ks:
                            mm = pe.matmul(PS[:, 2 * p + half, :], w[:, k, :], brT[:, k, half * 512:(half + 1) * 512],
                                           start=(k == ks[0]), stop=(k == ks[-1]))
                    mm.then_inc(weights_used[3] if br == 2 else psum_full[p], 1)
            pe.wait_ge(diag_made, KT * 2)
            pe.wait_ge(ones_made, 1)
            for r, dg in enumerate((diag, diag2)):
                p = L.pair("rows", r)
                pair_here(pe, "rows", 0, r)
                for half in range(2):
                    mm = pe.matmul(PS[:, 2 * p + half, :], ones[:, :], dg[:, half * 512:(half + 1) * 512],
                                   start=True, stop=True)
                mm.then_inc(psum_full[p], 1)
            pe.sem_inc(merged_split, 1)
            by_token_split(pe, "out2", mergedT_high, mergedT_low, (wo2_high, wo2_low),
                           lambda i, k: pe.wait_ge(merged_split, k + 2))
            turn(pe, "turn_h2", lambda b, k: xhat2[:, b % 2, k * P:(k + 1) * P],
                 lambda b: pe.wait_ge(xhat_made[1], b + 1))
            pe.wait_ge(h_made[1], NB)
            ffn(pe, 1, "ffn2", 2, h2T_high, h2T_low, (hid2_high, hid2_low), (w2_high, w2_low), DOWN2_PAIRS)

        def unit_here(name, eng, stage, i, u):
            kind, n, value = L.full(stage, i, u)
            hold(name, eng, {"weights_used": weights_used, "parts_used": parts_used, "psum_full": psum_full}[kind][n],
                 value)

        def copy_turned(act, stage, dest):
            for b in range(NB):
                p = L.pair(stage, b)
                unit_here("act", act, stage, 0, b)
                act.copy(dest[:, :, tok(b)], flat(p).rearrange("p (k n) -> p k n", k=KT)).then_inc(psum_free[p], 1)

        def high_turned(act, stage, dest, made):
            for b in range(NB):
                unit_here("act", act, stage, 0, b)
                act.copy(dest[:, :, tok(b)], flat(L.pair(stage, b)).rearrange("p (k n) -> p k n", k=KT)
                         ).then_inc(made, 1)

        def copy_features(act, stage, dest, at=0):
            n = len(L.units[stage])
            with loop(act, L.iters[stage]) as i:
                for c in range(n):
                    p = L.pair(stage, c)
                    unit_here("act", act, stage, i, c)
                    act.copy(dest[:, bass.ds(n * i + c + at, 1), :].rearrange("p a n -> p (a n)"), flat(p)
                             ).then_inc(psum_free[p], 1)

        def square_sums(act, r, source, waits):
            for b in range(NB):
                waits(b)
                act.activation(junks[r], source[:, b, :], ACT.Square, accum_out=ssq[:, b:b + 1]).then_inc(act_chain, 1)
                act_links[0] += 1
                act.wait_ge(act_chain, act_links[0])
            act.wait_ge(act_chain, act_links[0])
            act.sem_inc(rms_sum[r], 1)
            act.wait_ge(rms_var[r], 1)
            act.activation(rstd[:, :], rstd[:, :], ACT.Sqrt).then_inc(rms_sqrt[r], 1)

        act_links = [0]

        def layer_norm_act(act, r):
            act.wait_ge(ln_var[r], 1)
            act.activation(rstd[:, :], rstd[:, :], ACT.Sqrt).then_inc(ln_sqrt[r], 1)
            act.wait_ge(ln_sqrt[r], 2)
            for b in range(NB):
                act.activation(y1[:, b, :], y1[:, b, :], ACT.Identity, bias=nmr[:, b:b + 1],
                               scale=rstd[:, b:b + 1]).then_inc(ln_scaled[r], 1)

        def modulated_act(act, r, xhat, source, stage, shaped, h_high):
            act.wait_ge(rms_rstd[2 * r], 1)
            for b in range(NB + 2):
                if b >= 2:
                    unit_here("act", act, stage, 0, b - 2)
                if b < NB:
                    act.activation(xhat[:, b % 2, :], source[:, b, :], ACT.Copy, scale=rstd[:, b:b + 1]
                                   ).then_inc(xhat_made[r], 1)
                if b >= 2:
                    act.wait_ge(h_shifted[r], b - 1)
                    act.copy(h_high[:, :, tok(b - 2)], shaped[:, b % 2, :, :]).then_inc(h_high_made[r], 1)

        @block.scalar
        def _(act):
            act.wait_ge(consts_loaded, 16 * N_CONSTS)
            act.activation(c_act[:, :], c_col[:, :], ACT.Silu).then_inc(c_act_made, 1)
            act.wait_ge(lam_sums, 2)
            act.activation(lam_e[:, :], lam_s[:, :], ACT.Exp).then_inc(lam_exps, 1)
            copy_turned(act, "turn_x", xT)
            copy_features(act, "cqk", cqkT)
            for c in range(3):
                p = L.pair("idx", c)
                unit_here("act", act, "idx", 0, c)
                act.copy(iqT[:, c, :] if c < 2 else ikT[:, :], flat(p)).then_inc(psum_free[p], 1)
            for p in range(4):
                unit_here("act", act, "cv", 0, p)
                act.copy(cvw[:, 2 * p:2 * p + 2, :], pair(p)[:, :, 0:264]).then_inc(psum_free[p], 1)
            for p in range(4):
                unit_here("act", act, "auv", 0, p)
                act.activation(au[:, 2 * p:2 * p + 2, :], pair(p)[:, :, 0:256], ACT.Gelu_apprx_tanh
                               ).then_inc(act_chain, 1)
                act_links[0] += 1
                act.activation(av[:, 2 * p:2 * p + 2, :], pair(p)[:, :, 256:512], ACT.Gelu_apprx_tanh
                               ).then_inc(psum_free[p], 1)
            act.wait_ge(act_chain, act_links[0])
            act.wait_ge(gmlp_var, 1)
            act.activation(vstat[:, 1, :], vstat[:, 1, :], ACT.Sqrt).then_inc(gmlp_sqrt, 1)
            for n, (b, h) in enumerate(SCORE_UNITS):
                p = L.pair("score", n)
                unit_here("act", act, "score", 0, n)
                if n >= 2:
                    act.wait_ge(score_added, n - 1)
                act.activation(relu[:, n % 2, 0:P * (b + 1)], flat(p)[:, 0:P * (b + 1)], ACT.Relu
                               ).then_inc(psum_free[p], 1)
            copy_features(act, "bqk", bqkT)
            for p in range(4):
                unit_here("act", act, "bv", 0, p)
                act.copy(bv[:, 2 * p:2 * p + 2, :], pair(p)).then_inc(psum_free[p], 1)
            act.wait_ge(score_added, len(SCORE_UNITS))
            diff.act(act)
            act.wait_ge(o_var, 1)
            act.activation(o_ssq[:, :], o_ssq[:, :], ACT.Sqrt).then_inc(o_sqrt, 1)
            sparse.act(act)
            high_turned(act, "turn_mix", mixT_high, mix_high_made)
            layer_norm_act(act, 0)
            high_turned(act, "turn_x1", x1T_high, x1_high_made)
            with act.Fori(0, FT // 2) as i:
                for j in range(2):
                    g, u = L.pair("ffn1", 2 * j), L.pair("ffn1", 2 * j + 1)
                    unit_here("act", act, "ffn1", i, 2 * j)
                    hold("act", act, hid_made[0], 2 * i + (j + 1))
                    act.activation(silu_t[:, j, :], flat(g), ACT.Silu).then_inc(psum_free[g], 1)
                    hold("act", act, psum_free[u], L.pair_uses("ffn1", i, 2 * j + 1) + 1)
                    act.copy(hid1_high[:, j, :], silu_t[:, j, :]).then_inc(hid_high[0], 1)
            layer_norm_act(act, 1)
            square_sums(act, 0, y1, lambda b: act.wait_ge(ln_tile[1], b + 1))
            modulated_act(act, 0, xhat, y1, "turn_h", shaped, hT_high)
            copy_features(act, "qk2", qk2T)
            for p in range(4):
                unit_here("act", act, "v2", 0, p)
                act.copy(v2[:, 2 * p:2 * p + 2, :], pair(p)).then_inc(psum_free[p], 1)
            act.wait_ge(fl_exp, 1)
            act.activation(lsf_b[0:8, :], lsf_b[0:8, :], ACT.Exp, scale=-1.0).then_inc(act_chain, 1)
            act_links[0] += 1
            act.wait_ge(act_chain, act_links[0])
            act.activation(lsf_b[0:8, :], lsf_b[0:8, :], ACT.Ln, bias=1.0).then_inc(fl_ln, 1)
            copy_features(act, "z2", z2T)
            act.wait_ge(cum_done, 1)
            for h in range(8):
                p = L.pair("spread_cum", h)
                unit_here("act", act, "spread_cum", 0, h)
                act.activation(negcum[:, h, :], flat(p), ACT.Copy, scale=-8.0).then_inc(psum_free[p], 1)
            act.wait_ge(br_bc_made, 4)
            forget.act(act)
            with act.Fori(0, KT) as i:
                for c in range(3):
                    p, q = L.pair("branch", c), L.pair("branch", 3 + c)
                    unit_here("act", act, "branch", i, c)
                    hold("act", act, psum_free[q], L.pair_uses("branch", i, 3 + c))
                    act.activation(sig[:, c, :], flat(p), ACT.Sigmoid).then_inc(psum_free[p], 1)
            for k in range(KT):
                act.wait_ge(merged_step, 1 + 2 * KT)
                act.copy(mergedT_high[:, k, :], mergedT[:, k, :]).then_inc(merged_high_made, 1)
            for r, dest in enumerate((row_gain, row_gain2)):
                p = L.pair("rows", r)
                unit_here("act", act, "rows", 0, r)
                act.copy(dest, flat(p)).then_inc(psum_free[p], 1)
            square_sums(act, 1, y2, lambda b: all_pairs_free(act, "turn_h2"))
            act.wait_ge(rms_rstd[1], 1)
            for b in range(NB):
                act.activation(y2[:, b, :], y2[:, b, :], ACT.Copy, scale=rstd[:, b:b + 1]).then_inc(y2_scaled, 1)
            act.wait_ge(y2_scaled, NB)
            square_sums(act, 2, y2, lambda b: act.wait_ge(x3_made, b + 1))
            modulated_act(act, 1, xhat2, y2, "turn_h2", shaped2, h2T_high)
            with act.Fori(0, FFT // 2) as i:
                for j in range(2):
                    p = L.pair("ffn2", j)
                    unit_here("act", act, "ffn2", i, j)
                    hold("act", act, hid_made[1], 2 * i + (j + 1))
                    act.activation(relu_t[:, j, :], flat(p), ACT.Relu).then_inc(psum_free[p], 1)
                    hold("act", act, hid_squared, 2 * i + (j + 1))
                    act.copy(hid2_high[:, j, :], relu_t[:, j, :]).then_inc(hid_high[1], 1)
            square_sums(act, 3, y3, lambda b: all_pairs_free(act, "end"))
            act.wait_ge(rms_rstd[3], 1)
            for b in range(NB):
                act.activation(y3[:, b, :], y3[:, b, :], ACT.Copy, scale=rstd[:, b:b + 1]).then_inc(y3_scaled, 1)

        links = [0]

        def add_scaled(dve, stage, dest, source):
            with dve.Fori(0, 2) as i:
                for p in range(4):
                    unit_here("dve", dve, stage, i, p)
                    where = (slice(None), slice(2 * p, 2 * p + 2), bass.ds(512 * i, 512))
                    dve.scalar_tensor_tensor(out=dest[where], in0=source[where], scalar=ALPHA, in1=pair(p),
                                             op0=ALU.mult, op1=ALU.add).then_inc(psum_free[p], 1)

        def low_hidden(dve, r, i, j, hidden, hid_parts):
            hold("dve", dve, hid_high[r], 2 * i + (j + 1))
            dve.tensor_tensor(hid_parts[1][:, j, :], hidden[:, j, :], hid_parts[0][:, j, :].bitcast(F32), ALU.subtract
                              ).then_inc(hid_made[r], 1)

        def add_halves(dve, stage, i, tiles, dest, down_pairs):
            for half in range(2):
                for at, p in enumerate(down_pairs[half]):
                    unit_here("dve", dve, stage, i, tiles + 4 * half + at)
                    where = dest[:, 2 * p:2 * p + 2, half * 512:(half + 1) * 512]
                    dve.tensor_tensor(where, where, pair(p), ALU.add).then_inc(psum_free[p], 1)

        def low_turned(dve, stage, high, low, made):
            for b in range(NB):
                p = L.pair(stage, b)
                dve.wait_ge(made, b + 1)
                dve.tensor_tensor(low[:, :, tok(b)], flat(p).rearrange("p (k n) -> p k n", k=KT),
                                  high[:, :, tok(b)].bitcast(F32), ALU.subtract).then_inc(psum_free[p], 1)

        def layer_norm_dve(dve, do, link, r):
            all_pairs_free(dve, ("turn_x1", "turn_h")[r])
            for b in range(NB):
                for half in range(2):
                    do(dve.bn_stats(bn[:, 6 * half:6 * half + 6], y1[:, b, half * 512:(half + 1) * 512]))
                do(dve.bn_aggr(stats[:, 2 * b:2 * b + 2], bn[:, :]))
            st = stats[:, :].rearrange("p (b c) -> p b c", c=2)
            dve.tensor_scalar(rstd[:, :], st[:, :, 1], EPS_LN, None, ALU.add).then_inc(ln_var[r], 1)
            dve.wait_ge(ln_sqrt[r], 1)
            do(dve.reciprocal(rstd[:, :], rstd[:, :]))
            dve.scalar_tensor_tensor(out=nmr[:, :], in0=st[:, :, 0], scalar=-1.0, in1=rstd[:, :],
                                     op0=ALU.mult, op1=ALU.mult).then_inc(ln_sqrt[r], 1)
            dve.wait_ge(ln_rows_loaded[r], 32)
            for b in range(NB):
                dve.wait_ge(ln_scaled[r], b + 1)
                dve.tensor_tensor(y1[:, b, :], y1[:, b, :], ln_g, ALU.mult).then_inc(ln_gained[r], 1)

        def rms_dve(dve, do, r):
            dve.wait_ge(rms_sum[r], 1)
            dve.tensor_scalar(rstd[:, :], ssq[:, :], 1.0 / D, EPS_RMS, ALU.mult, ALU.add).then_inc(rms_var[r], 1)
            dve.wait_ge(rms_sqrt[r], 1)
            dve.reciprocal(rstd[:, :], rstd[:, :]).then_inc(rms_rstd[r], 1)

        def modulated_dve(dve, r, stage, shaped, gain, h_high, h_low):
            for b in range(NB + 1):
                if b < NB:
                    p = L.pair(stage, b)
                    unit_here("dve", dve, stage, 0, b)
                    if b >= 2:
                        dve.wait_ge(h_made[r], b - 1)
                    dve.tensor_tensor(shaped[:, b % 2, :, :], flat(p).rearrange("p (k n) -> p k n", k=KT),
                                      gain[:, :].unsqueeze(2).to_broadcast([P, KT, P]), ALU.mult
                                      ).then_inc(psum_free[p], 1)
                if b >= 1:
                    dve.wait_ge(h_high_made[r], b)
                    dve.tensor_tensor(h_low[:, :, tok(b - 1)], shaped[:, (b - 1) % 2, :, :],
                                      h_high[:, :, tok(b - 1)].bitcast(F32), ALU.subtract).then_inc(h_made[r], 1)

        @block.vector
        def _(dve):
            def link():
                links[0] += 1
                dve.wait_ge(dve_chain, links[0])

            def do(ins):
                ins.then_inc(dve_chain, 1)
                link()

            dve.wait_ge(dist_made, 1)
            do(dve.scalar_tensor_tensor(out=dist, in0=dist, scalar=-1.0, in1=dist, op0=ALU.mult, op1=ALU.max))
            for h in range(4):
                do(dve.tensor_scalar(bias8[:, h, :], dist, -8.0 * SLOPES[h], None, ALU.mult))
                dve.memset(bias8[0:64, h, S - 64:S], NEG).then_inc(bias_made, 1)
            dve.wait_ge(consts_loaded, 16 * N_CONSTS)
            for j in range(2):
                dve.tensor_tensor_reduce(out=vstat_lam[:, j, :], in0=lam_v[:, 2 * j, :], in1=lam_v[:, 2 * j + 1, :],
                                         scale=1.0, scalar=0.0, op0=ALU.mult, op1=ALU.add,
                                         accum_out=lam_s[:, j:j + 1]).then_inc(lam_sums, 1)
            dve.wait_ge(lam_exps, 1)
            do(dve.tensor_tensor(neglam[:, :], lam_e[:, 1:2], lam_e[:, 0:1], ALU.subtract))
            do(dve.tensor_scalar(neglam[:, :], neglam[:, :], -LAM_INIT, None, ALU.add))
            for p in range(4):
                dve.wait_ge(psum_free[p], L.pair_uses("cv", 0, p) + 1)
            do(dve.tensor_scalar(cvw[:, :, 256:264], cvw[:, :, 256:264], 1.0 / 16, None, ALU.mult))
            for p in range(4):
                dve.wait_ge(psum_free[p], L.pair_uses("auv", 0, p) + 1)
            unit_here("dve", dve, "turn_ws", 0, 0)
            dve.tensor_copy(wsT[:, :, :].rearrange("p g n -> p (g n)"), PS[:, 0, :]).then_inc(psum_free[0], 1)
            vg = av.rearrange("p b (g c) -> p (b g) c", c=64)

            def over(stat):
                return stat.unsqueeze(2).to_broadcast([P, NB * 4, 64])

            do(dve.tensor_reduce(vstat[:, 0, :], vg, AX.X, ALU.add))
            do(dve.tensor_scalar(vstat[:, 0, :], vstat[:, 0, :], 1.0 / 64, None, ALU.mult))
            do(dve.tensor_tensor(vg, vg, over(vstat[:, 0, :]), ALU.subtract))
            do(dve.tensor_tensor(v_sq, vg, vg, ALU.mult))
            do(dve.tensor_reduce(vstat[:, 1, :], v_sq, AX.X, ALU.add))
            dve.tensor_scalar(vstat[:, 1, :], vstat[:, 1, :], 1.0 / 64, EPS_LN, ALU.mult, ALU.add
                              ).then_inc(gmlp_var, 1)
            dve.wait_ge(gmlp_sqrt, 1)
            do(dve.reciprocal(vstat[:, 2, :], vstat[:, 1, :]))
            do(dve.tensor_tensor(vg, vg, over(vstat[:, 2, :]), ALU.mult))
            do(dve.tensor_tensor(av, av, aln[:, 0:1, :].to_broadcast([P, NB, 256]), ALU.mult))
            dve.tensor_tensor(av, av, aln[:, 1:2, :].to_broadcast([P, NB, 256]), ALU.add).then_inc(v_normed, 1)
            for n, (b, h) in enumerate(SCORE_UNITS):
                N = P * (b + 1)
                dve.wait_ge(psum_free[L.pair("score", n)], L.pair_uses("score", 0, n) + 1)
                wcol = cvw[:, b, 256 + h:257 + h]
                if h == 0:
                    dve.tensor_scalar(score[b], relu[:, n % 2, 0:N], wcol, None, ALU.mult).then_inc(score_added, 1)
                else:
                    dve.wait_ge(score_added, n)
                    dve.scalar_tensor_tensor(out=score[b], in0=relu[:, n % 2, 0:N], scalar=wcol, in1=score[b],
                                             op0=ALU.mult, op1=ALU.add).then_inc(score_added, 1)
            for g in range(4):
                if g % 2 == 0:
                    unit_here("dve", dve, "gmlp", 0, g // 2)
                ug = au[:, :, g * 64:(g + 1) * 64]
                ins = dve.scalar_tensor_tensor(out=ug, in0=PS[:, g, :].rearrange("p (b c) -> p b c", c=64),
                                               scalar=bs_col[:, g:g + 1], in1=ug, op0=ALU.add, op1=ALU.mult)
                ins.then_inc(psum_free[g // 2] if g % 2 else dve_chain, 1)
                if g % 2 == 0:
                    link()
            dve.wait_ge(score_added, len(SCORE_UNITS))
            blocks = range(2, NB)
            for b in blocks:
                dve.memset(score[b][0:64, P * b + 64:P * b + P], FORBIDDEN).then_inc(topk_step, 1)
            nb = len(blocks)

            def largest(i):
                for b in blocks:
                    hold("dve", dve, topk_step, 2 * nb * i + b - 1)
                    dve.max(top8[:, 8 * (b - 2):8 * (b - 1)], score[b]).then_inc(topk_step, 1)

            def strike(i):
                for b in blocks:
                    hold("dve", dve, topk_step, nb + 2 * nb * i + b - 1)
                    dve.match_replace(out=score[b], in_to_replace=top8[:, 8 * (b - 2):8 * (b - 1)],
                                      in_values=score[b], imm_value=TAKEN).then_inc(topk_step, 1)

            rounds = TOPK // 8
            early = rounds - len(heads4) // 2
            with dve.Fori(0, early) as i:
                largest(i)
                strike(i)
            for p in range(4):
                dve.wait_ge(psum_free[p], L.pair_uses("bv", 0, p) + 1)
            diff.dve(dve, link, lambda u: (largest, strike)[u % 2](early + u // 2))
            dve.wait_ge(topk_step, nb + 2 * nb * rounds)
            for b in blocks:
                dve.tensor_scalar(mask[b], score[b], -2e38, NEG, ALU.is_gt, ALU.mult).then_inc(topk_done, 1)
            o_heads = [mix[:, b, 0:512].rearrange("p (h e) -> p h e", e=P) for b in range(NB)]
            for half in range(2):
                for b in range(4 * half, 4 * half + 4):
                    do(dve.tensor_tensor(o_sq[:, 4 * (b % 4):4 * (b % 4) + 4, :], o_heads[b], o_heads[b], ALU.mult))
                do(dve.tensor_reduce(o_ssq[:, 16 * half:16 * half + 16], o_sq[:, 0:16, :], AX.X, ALU.add))
            dve.tensor_scalar(o_ssq[:, :], o_ssq[:, :], 1.0 / P, EPS_LN, ALU.mult, ALU.add).then_inc(o_var, 1)
            dve.wait_ge(o_sqrt, 1)
            do(dve.reciprocal(o_ssq[:, :], o_ssq[:, :]))
            do(dve.tensor_scalar(o_ssq[:, :], o_ssq[:, :], 1.0 - LAM_INIT, None, ALU.mult))
            for b in range(NB):
                do(dve.tensor_tensor(o_heads[b], o_heads[b],
                                     o_ssq[:, 4 * b:4 * b + 4].unsqueeze(2).to_broadcast([P, 4, P]), ALU.mult))
                do(dve.tensor_tensor(o_heads[b], o_heads[b],
                                     subln.unsqueeze(1).to_broadcast([P, 4, P]), ALU.mult))
            sparse.dve(dve, link)
            dve.wait_ge(ada_done, 1)
            do(dve.tensor_tensor(mod[:, :], PS[:, 7, 0:N_ADA], b_ada[:, :], ALU.add))
            dve.sem_inc(mix_done, 1)
            for gain, k, g in ((gain_m, 1, g_mix_pre), (gain_f, 4, g_ff_pre)):
                do(dve.scalar_tensor_tensor(out=gain[:, :], in0=mod[:, KT * k:KT * k + KT], scalar=1.0, in1=g[:, :],
                                            op0=ALU.add, op1=ALU.mult))
            for gate, k, g in ((gate_m, 2, g_mix_post), (gate_f, 5, g_ff_post)):
                do(dve.tensor_tensor(gate[:, :], mod[:, KT * k:KT * k + KT], g[:, :], ALU.mult))
            dve.sem_inc(mod_made, 1)
            low_turned(dve, "turn_mix", mixT_high, mixT_low, mix_high_made)
            dve.wait_ge(xres_loaded, 16)
            add_scaled(dve, "out1", y1, x_res)
            layer_norm_dve(dve, do, link, 0)
            low_turned(dve, "turn_x1", x1T_high, x1T_low, x1_high_made)
            for b in range(NB):
                dve.tensor_scalar(y1[:, b, :], y1[:, b, :], ALPHA, None, ALU.mult).then_inc(y1_grown, 1)
            dve.wait_ge(y1_grown, NB)
            dve.sem_inc(hid_made[0], 2)
            with dve.Fori(0, FT // 2) as i:
                for j in range(2):
                    u = L.pair("ffn1", 2 * j + 1)
                    unit_here("dve", dve, "ffn1", i, 2 * j + 1)
                    hold("dve", dve, psum_free[L.pair("ffn1", 2 * j)], L.pair_uses("ffn1", i, 2 * j) + 1)
                    dve.tensor_tensor(silu_t[:, j, :], silu_t[:, j, :], flat(u), ALU.mult).then_inc(psum_free[u], 1)
                    low_hidden(dve, 0, i, j, silu_t, (hid1_high, hid1_low))
                add_halves(dve, "ffn1", i, 4, y1, DOWN1_PAIRS)
            layer_norm_dve(dve, do, link, 1)
            rms_dve(dve, do, 0)
            modulated_dve(dve, 0, "turn_h", shaped, gain_m, hT_high, hT_low)
            unit_here("dve", dve, "fl2", 0, 0)
            dve.wait_ge(x2_stored, 16)
            dve.tensor_scalar(lsf_a[0:8, :], flat(0)[0:8, :], b_f[0:8, 0:1], None, ALU.add).then_inc(psum_free[0], 1)
            dve.wait_ge(psum_free[0], L.pair_uses("fl2", 0, 0) + 1)
            dve.scalar_tensor_tensor(out=lsf_b[0:8, :], in0=lsf_a[0:8, :], scalar=-1.0, in1=lsf_a[0:8, :],
                                     op0=ALU.mult, op1=ALU.max).then_inc(fl_exp, 1)
            dve.wait_ge(fl_ln, 1)
            do(dve.scalar_tensor_tensor(out=lsf_a[0:8, :], in0=lsf_a[0:8, :], scalar=0.0, in1=lsf_b[0:8, :],
                                        op0=ALU.min, op1=ALU.subtract))
            do(dve.memset(lsf_b[0:8, :], 1.0))
            dve.tensor_tensor_scan(fl[0:8, :], lsf_b[0:8, :], lsf_a[0:8, :], 0.0, ALU.mult, ALU.add
                                   ).then_inc(cum_done, 1)
            unit_here("dve", dve, "turn_cum", 0, 0)
            dve.tensor_scalar(cumq8[:, :], PS[:, 0, 0:64], 8.0, None, ALU.mult).then_inc(psum_free[0], 1)
            dve.wait_ge(counts_made, 2)
            for g in range(2):
                for half in range(2):
                    r = slice(64 * half, 64 * half + 64)
                    do(dve.tensor_scalar(pool_inv[r, g, :], pool_inv[r, g, :], float(POOL_WINDOWS[2 * g + half]), None,
                                         ALU.min))
            do(dve.reciprocal(pool_inv, pool_inv))
            for p in range(4):
                dve.wait_ge(psum_free[p], L.pair_uses("z2", 1, p) + 1)
            dve.wait_ge(h_low_stored, 16)
            do(dve.memset(pad_a[:, 0:16], 0.0))
            do(dve.memset(pad_b[:, 0:16], 0.0))
            for g in range(2):
                do(dve.tensor_copy(pad_a[:, 16:16 + S], z2T[:, g, :]))
                src, dst, shift = pad_a, pad_b, 1
                for _ in range(1 + 2 * g):
                    do(dve.tensor_tensor(dst[:, 16:16 + S], src[:, 16:16 + S], src[:, 16 - shift:16 - shift + S], ALU.add))
                    src, dst, shift = dst, src, 2 * shift
                do(dve.tensor_tensor(dst[64:128, 16:16 + S], src[64:128, 16:16 + S],
                                     src[64:128, 16 - shift:16 - shift + S], ALU.add))
                for half, sums in enumerate((src, dst)):
                    r = slice(64 * half, 64 * half + 64)
                    w = POOL_WINDOWS[2 * g + half]
                    do(dve.tensor_tensor(sums[r, 16:32], sums[r, 16:32], pool_inv[r, g, :], ALU.mult))
                    do(dve.tensor_tensor(z2T[r, g, 0:16], sums[r, 16:32], z2T[r, g, 0:16], ALU.subtract))
                    do(dve.scalar_tensor_tensor(out=z2T[r, g, 16:S], in0=sums[r, 32:16 + S], scalar=1.0 / w,
                                                in1=z2T[r, g, 16:S], op0=ALU.mult, op1=ALU.subtract))
                dve.sem_inc(pooled, 1)
            for g in range(2):
                do(dve.tensor_tensor(pad_a[:, 16:16 + S], z2T[:, 6 + g, :], z2T[:, 2 + g, :], ALU.mult))
                do(dve.tensor_scalar(ps_t, pad_a[:, 16:16 + S], conv_w[:, 4 + g:5 + g], None, ALU.mult))
                for tap in (1, 0):
                    back = 2 - tap
                    do(dve.scalar_tensor_tensor(out=ps_t, in0=pad_a[:, 16 - back:16 - back + S],
                                                scalar=conv_w[:, 2 * tap + g:2 * tap + g + 1], in1=ps_t,
                                                op0=ALU.mult, op1=ALU.add))
                do(dve.tensor_tensor(brT[:, 6 + g, :], ps_t, z2T[:, 4 + g, :], ALU.mult))
                dve.sem_inc(br_bc_made, 1)
            for g in range(2):
                unit_here("dve", dve, "pool", 0, g)
                dve.tensor_scalar(brT[:, 4 + g, :], flat(g), pscale[:, g:g + 1], None, ALU.mult
                                  ).then_inc(psum_free[g], 1)
                dve.wait_ge(psum_free[g], L.pair_uses("pool", 0, g) + 1)
                dve.sem_inc(br_bc_made, 1)
            forget.dve(dve, link)
            dve.sem_inc(merged_step, 1)
            with dve.Fori(0, KT) as i:
                for c in range(3):
                    p, q = L.pair("branch", c), L.pair("branch", 3 + c)
                    unit_here("dve", dve, "branch", i, 3 + c)
                    hold("dve", dve, psum_free[p], L.pair_uses("branch", i, c) + 1)
                    hold("dve", dve, merged_step, 2 * i + 1 + (c == 2))
                    dve.tensor_tensor(mg[:, min(c, 1), :], sig[:, c, :], flat(q), ALU.mult).then_inc(psum_free[q], 1)
                    if c == 0:
                        continue
                    hold("dve", dve, psum_free[q], L.pair_uses("branch", i, 3 + c) + 1)
                    dest = mg[:, 0, :] if c == 1 else mergedT[:, bass.ds(i, 1), :].rearrange("p a n -> p (a n)")
                    dve.tensor_tensor(dest, mg[:, 0, :], mg[:, 1, :], ALU.add).then_inc(merged_step, 1)
            for k in range(KT):
                dve.wait_ge(merged_high_made, k + 1)
                dve.tensor_tensor(mergedT_low[:, k, :], mergedT[:, k, :], mergedT_high[:, k, :].bitcast(F32),
                                  ALU.subtract).then_inc(merged_split, 1)
            for dg, gate in ((diag, gate_m), (diag2, gate_f)):
                for k in range(KT):
                    dve.tensor_scalar(dg[:, k * P:(k + 1) * P], ident[:, :], gate[:, k:k + 1], None, ALU.mult
                                      ).then_inc(diag_made, 1)
            with dve.Fori(0, 2) as i:
                for p in range(4):
                    unit_here("dve", dve, "out2", i, p)
                    dve.tensor_copy(y2[:, 2 * p:2 * p + 2, bass.ds(512 * i, 512)], pair(p)).then_inc(psum_free[p], 1)
            rms_dve(dve, do, 1)
            dve.wait_ge(x2_back, 32)
            for r in range(2):
                dve.wait_ge(psum_free[L.pair("rows", r)], L.pair_uses("rows", 0, r) + 1)
            for b in range(NB):
                dve.wait_ge(y2_scaled, b + 1)
                do(dve.tensor_tensor(y2[:, b, :], y2[:, b, :], row_gain, ALU.mult))
                dve.tensor_tensor(y2[:, b, :], y2[:, b, :], x2_res[:, b, :], ALU.add).then_inc(x3_made, 1)
            rms_dve(dve, do, 2)
            modulated_dve(dve, 1, "turn_h2", shaped2, gain_f, h2T_high, h2T_low)
            dve.wait_ge(y3_zeroed, 1)
            dve.sem_inc(hid_made[1], 2)
            with dve.Fori(0, FFT // 2) as i:
                for j in range(2):
                    hold("dve", dve, psum_free[L.pair("ffn2", j)], L.pair_uses("ffn2", i, j) + 1)
                    dve.tensor_tensor(relu_t[:, j, :], relu_t[:, j, :], relu_t[:, j, :], ALU.mult
                                      ).then_inc(hid_squared, 1)
                    low_hidden(dve, 1, i, j, relu_t, (hid2_high, hid2_low))
                add_halves(dve, "ffn2", i, 2, y3, DOWN2_PAIRS)
            rms_dve(dve, do, 3)
            for b in range(NB):
                dve.wait_ge(y3_scaled, b + 1)
                do(dve.tensor_tensor(y3[:, b, :], y3[:, b, :], row_gain2, ALU.mult))
                dve.tensor_tensor(y3[:, b, :], y3[:, b, :], y2[:, b, :], ALU.add).then_inc(out_made, 1)

        def shift(pool, r, shaped, col, stage):
            for b in range(NB):
                pool.wait_ge(psum_free[L.pair(stage, b)], L.pair_uses(stage, 0, b) + 1)
                pool.tensor_tensor(shaped[:, b % 2, :, :], shaped[:, b % 2, :, :],
                                   col.unsqueeze(2).to_broadcast([P, KT, P]), ALU.add).then_inc(h_shifted[r], 1)

        def split_weights(pool, stage, w_high, w_low):
            n = SPLIT[stage][0]
            with loop(pool, L.iters[stage]) as i:
                for c in range(n):
                    s, q = L.slot(stage, c), L.parts_slot(stage, c)
                    hold("pool", pool, weights_loaded[s], L.loaded(stage, i, c))
                    hold("pool", pool, parts_used[q], L.parts_uses(stage, i, c))
                    pool.tensor_scalar(w_high[:, q, :], ring[:, s, :], 1.0, 1.0, ALU.mult, ALU.mult
                                       ).then_inc(weights_high, 1)
                    hold("pool", pool, weights_high, L.high_base[stage] + n * i + (c + 1))
                    pool.tensor_tensor(w_low[:, q, :], ring[:, s, :], w_high[:, q, :].bitcast(F32),
                                       ALU.subtract).then_inc(weights_used[s], 1)

        @block.gpsimd
        def _(pool):
            loads = 0

            def load(dst, src):
                nonlocal loads
                with nc.allow_non_contiguous_dma(reason="small constants"):
                    pool.dma_start(dst, src).then_inc(consts_loaded, 16)
                loads += 1

            def column(name, width=P):
                return t[name].rearrange("a (k p) -> p (a k)", p=width)

            links = [0]

            def do(ins):
                links[0] += 1
                ins.then_inc(pool_chain, 1)
                pool.wait_ge(pool_chain, links[0])

            do(pool.memset(ident[:, :], 0.0))
            pool.affine_select(out=ident[:, :], in_=ident[:, :], compare_op=ALU.not_equal, fill=1.0, base=0,
                               pattern=[[-1, P]], channel_multiplier=1).then_inc(ident_made, 1)
            do(pool.memset(causal8[:, :], 0.0))
            pool.affine_select(out=causal8[:, :], in_=causal8[:, :], compare_op=ALU.is_ge, fill=NEG, base=0,
                               pattern=[[-1, P]], channel_multiplier=1).then_inc(ident_made, 1)
            pool.iota(dist, pattern=[[-1, S]], base=S - P, channel_multiplier=1,
                      allow_small_or_imprecise_dtypes=True).then_inc(dist_made, 1)
            load(c_col[:, :], column("c_2"))
            load(b_ada[:, :], column("b_ada_2"))
            for dst, name in ((g_mix_pre, "g_mix_pre_2"), (g_ff_pre, "g_ff_pre_2"), (g_mix_post, "g_mix_post_2"),
                              (g_ff_post, "g_ff_post_2"), (pscale, "pool_scale_2")):
                load(dst[:, :], column(name))
            load(conv_w[:, :], t["conv_w_2"].rearrange("a t (g p) -> p (a t g)", p=P))
            load(b_f[0:8, :], t["b_f_2"].rearrange("a h -> h a"))
            load(bs_col[:, :], t["gmlp_b_s"].rearrange("a g n -> n (a g)"))
            for j, name in enumerate(("lam_q1", "lam_k1", "lam_q2", "lam_k2")):
                load(lam_v[:, j, :], t[name].to_broadcast([P, 64]))
            load(subln, t["diff_subln_g"].to_broadcast([P, P]))
            for j, name in enumerate(("gmlp_ln_g", "gmlp_ln_b")):
                load(aln[:, j, :], t[name].rearrange("a g c -> a (g c)").to_broadcast([P, 256]))
            assert loads == N_CONSTS
            pool.dma_start(ws_tok, t["gmlp_w_s"].rearrange("a g t s -> t (a g) s")).then_inc(ws_loaded, 16)
            pool.wait_ge(ws_loaded, 16)
            pool.memset(ws_tok[0:64, :, 64:128], 0.0).then_inc(ws_masked, 1)
            pool.memset(pool_w[:, :, :], 0.0).then_inc(pool_w_zeroed, 1)
            pool.wait_ge(pool_w_zeroed, 1)
            for g in range(4):
                r = slice(64 * (g % 2), 64 * (g % 2) + 64)
                pool.dma_start(pool_w[r, g // 2, r], t["w_pool_2"][0, g]).then_inc(pool_w_loaded, 16)
            pool.wait_ge(topk_done, NB - 2)
            k = 0
            for u, (h, b) in enumerate(heads4):
                if b < 2:
                    continue
                if k >= 2:
                    prev = [v for v, (_, bb) in enumerate(heads4) if bb >= 2][k - 2]
                    pool.wait_ge(sparse.logits_made, prev + 1)
                pool.tensor_tensor(cbias[:, k % 2, 0:P * (b + 1)], bias8[:, h, P * (NB - 1 - b):S], mask[b], ALU.add
                                   ).then_inc(cbias_made, 1)
                k += 1
            pool.wait_ge(sparse.out_stored, len(heads4))
            pool.dma_start(x_res, t["x"][0].rearrange("(b p) d -> p b d", p=P)).then_inc(xres_loaded, 16)
            for r, (g, b) in enumerate((("ln1_g", "ln1_b"), ("ln2_g", "ln2_b"))):
                pool.dma_start(ln_g, t[g].to_broadcast([P, D])).then_inc(ln_rows_loaded[r], 16)
                pool.dma_start(ln_b, t[b].to_broadcast([P, D])).then_inc(ln_rows_loaded[r], 16)
                if r == 0:
                    split_weights(pool, "out1", wo1_high, wo1_low)
                pool.wait_ge(ln_rows_loaded[r], 32)
                for n in range(NB):
                    pool.wait_ge(ln_gained[r], n + 1)
                    pool.tensor_tensor(y1[:, n, :], y1[:, n, :], ln_b, ALU.add).then_inc(ln_tile[r], 1)
                pool.wait_ge(ln_tile[r], NB)
                if r == 0:
                    split_weights(pool, "ffn1", w1_high, w1_low)
            pool.dma_start(x2_dram.rearrange("(b p) d -> p b d", p=P), y1).then_inc(x2_stored, 16)
            shift(pool, 0, shaped, mod[:, 0:KT], "turn_h")
            pool.wait_ge(x2_stored, 16)
            for stage in ("qk2", "v2", "fl2", "z2"):
                split_weights(pool, stage, win2_high, win2_low)
                if stage == "qk2":
                    pool.wait_ge(h_made[0], NB)
                    pool.dma_start(h_low_dram, hT_low[:, :, :]).then_inc(h_low_stored, 16)
            for g in range(2):
                pool.iota(pool_inv[:, g, :], pattern=[[1, 16]], base=1, channel_multiplier=0,
                          allow_small_or_imprecise_dtypes=True).then_inc(counts_made, 1)
            do(pool.memset(selw[0:8, :, :], 1.0))
            pool.affine_select(out=selw[0:8, :, :], in_=selw[0:8, :, :], compare_op=ALU.is_equal, fill=0.0, base=0,
                               pattern=[[-1, 8], [0, P]], channel_multiplier=1).then_inc(selw_made, 1)
            pool.wait_ge(psum_free[0], L.pair_uses("turn_cum", 0, 0) + 1)
            for p in range(4):
                pool.wait_ge(psum_free[p], L.pair_uses("spread_cum", 0, p + 4) + 1)
            pool.wait_ge(br_bc_made, 4)
            for u, (h, b) in enumerate(heads8):
                N = P * (b + 1)
                if u >= 2:
                    pool.wait_ge(forget.logits_made, u - 1)
                pool.tensor_scalar(fbias[:, u % 2, 0:N], negcum[:, h, 0:N], cumq8[:, 8 * b + h:8 * b + h + 1], None,
                                   ALU.add).then_inc(fbias_made, 1)
                pool.wait_ge(fbias_made, 2 * u + 1)
                pool.tensor_tensor(fbias[:, u % 2, N - P:N], fbias[:, u % 2, N - P:N], causal8[:, :], ALU.add
                                   ).then_inc(fbias_made, 1)
                if b == NB - 1:
                    pool.wait_ge(fbias_made, 2 * u + 2)
                    if h == 0:
                        pool.wait_ge(h_low_stored, 16)
                    pool.dma_start(hT_low_back[:, h, :], h_low_dram[:, h, :]).then_inc(h_low_back, 16)
            pool.wait_ge(forget.out_stored, len(heads8))
            split_weights(pool, "branch", wbr_high, wbr_low)
            pool.wait_ge(merged_step, 1 + 2 * KT)
            do(pool.memset(ones, 1.0))
            pool.sem_inc(ones_made, 1)
            x2_view = x2_dram.rearrange("(b p) d -> p b d", p=P)
            pool.dma_start(x2_res[:, 0:4, :], x2_view[:, 0:4, :]).then_inc(x2_back, 16)
            split_weights(pool, "out2", wo2_high, wo2_low)
            for q in range(2):
                pool.wait_ge(parts_used[q], L.parts_base["turn_h2"][q])
            pool.dma_start(x2_res[:, 4:8, :], x2_view[:, 4:8, :]).then_inc(x2_back, 16)
            pool.wait_ge(x3_made, NB)
            pool.memset(y3, 0.0).then_inc(y3_zeroed, 1)
            shift(pool, 1, shaped2, mod[:, 3 * KT:4 * KT], "turn_h2")
            split_weights(pool, "ffn2", w2_high, w2_low)

        @block.sync
        def _(sp):
            w1, w2 = t["w_in"][0], t["w_in_2"][0]

            def slot_free(stage, i, c):
                hold("sp", sp, weights_used[L.slot(stage, c)], L.slot_uses(stage, i, c))

            def load(stage, c, dst, src):
                sp.dma_start(dst, src).then_inc(weights_loaded[L.slot(stage, c)], 16)

            def feature_tiles(stage, w, column, width=P):
                rows = w.rearrange("(k p) n -> p k n", p=P)
                with loop(sp, L.iters[stage]) as i:
                    for c in range(len(L.slots[stage])):
                        slot_free(stage, i, c)
                        load(stage, c, ring[:, L.slot(stage, c), 0:KT * width].rearrange("p (k n) -> p k n", k=KT),
                             rows[:, :, bass.ds(column(i, c), width)])

            def token_tiles(stage, w, at=0):
                rows = w.rearrange("(k p) n -> p k n", p=P)
                with loop(sp, L.iters[stage]) as i:
                    for c in range(len(L.slots[stage])):
                        slot_free(stage, i, c)
                        load(stage, c, ring[:, L.slot(stage, c), :].rearrange("p (k n) -> p k n", k=2),
                             rows[:, 2 * c:2 * c + 2, bass.ds(i * 512 + at, 512)])

            def ffn_tiles(stage, tiles, w_up, w_down, column):
                rows_up = w_up.rearrange("(k p) n -> p k n", p=P)
                rows_down = w_down.rearrange("(i k p) n -> p i k n", p=P, k=2)
                with sp.Fori(0, L.iters[stage]) as i:
                    for c in range(tiles + 2):
                        slot_free(stage, i, c)
                        dst = ring[:, L.slot(stage, c), :]
                        if c < tiles:
                            load(stage, c, dst.rearrange("p (k n) -> p k n", k=KT),
                                 rows_up[:, :, bass.ds(column(i, c), P)])
                        else:
                            half = c - tiles
                            load(stage, c, dst.rearrange("p (a k n) -> p a k n", a=1, k=2),
                                 rows_down[:, bass.ds(i, 1), :, half * 512:(half + 1) * 512])

            for b in range(NB):
                sp.dma_start(x_tok[:, b, :], t["x"][0, tok(b), :]).then_inc(x_loaded[b], 16)
            feature_tiles("cqk", w1, lambda i, c: C_Q + c * P)
            rows = w1.rearrange("(k p) n -> p k n", p=P)
            for c in range(3):
                s = L.slot("idx", c)
                slot_free("idx", 0, c)
                dst = ring[:, s, :].rearrange("p (k n) -> p k n", k=KT)
                if c < 2:
                    load("idx", c, dst, rows[:, :, I_Q + c * P:I_Q + (c + 1) * P])
                else:
                    for r in range(4):
                        load("idx", c, dst[:, :, 32 * r:32 * r + 32], rows[:, :, I_K:I_K + 32])
            for c in range(4):
                slot_free("cv", 0, c)
                dst = ring[:, L.slot("cv", c), 0:528].rearrange("p (k n) -> p k n", k=2)
                load("cv", c, dst[:, :, 0:256], rows[:, 2 * c:2 * c + 2, C_V:C_V + 256])
                load("cv", c, dst[:, :, 256:264], rows[:, 2 * c:2 * c + 2, I_W:I_W + 8])
            token_tiles("auv", w1, A_U)
            feature_tiles("bqk", w1, lambda i, c: i * 512 + (B_Q + c * P))
            token_tiles("bv", w1, B_V)
            ada_rows = t["w_ada_2"][0].rearrange("(k p) n -> p k n", p=P)
            for j in range(N_ADA):
                slot_free("ada", 0, j)
                load("ada", j, ring[:, j % 4, :].rearrange("p (k n) -> p k n", k=KT), ada_rows[:, :, j * P:(j + 1) * P])
            token_tiles("out1", t["w_out"][0])
            ffn_tiles("ffn1", 4, t["w_gu"][0], t["w_down"][0], lambda i, c: i * 256 + ((c // 2) * P + (c % 2) * FH))
            feature_tiles("qk2", w2, lambda i, c: i * 512 + c * P)
            token_tiles("v2", w2, V2)
            feature_tiles("fl2", w2, lambda i, c: FL2)
            feature_tiles("z2", w2, lambda i, c: i * 512 + (Z2 + c * P))
            gates = w2.rearrange("(k p) n -> p k n", p=P)
            branches = t["w_branch_2"][0].rearrange("(k p) n -> p k n", p=P)
            with sp.Fori(0, KT) as i:
                for c in range(4):
                    slot_free("branch", i, c)
                    src = branches[:, :, bass.ds(i * P, P)] if c == 3 else gates[:, :, bass.ds(i * P + (GL2 + c * D), P)]
                    load("branch", c, ring[:, c, :].rearrange("p (k n) -> p k n", k=KT), src)
            token_tiles("out2", t["w_out_2"][0])
            ffn_tiles("ffn2", 2, t["w_ff1_2"][0], t["w_ff2_2"][0], lambda i, c: i * 256 + c * P)
            for b in range(NB):
                sp.wait_ge(out_made, b + 1)
                sp.dma_start(out[0, tok(b), :], y3[:, b, :]).then_inc(out_stored, 16)
            sp.wait_ge(out_stored, 16 * NB)


_INS = ['x', 'w_in', 'gmlp_w_s', 'gmlp_b_s', 'gmlp_ln_g', 'gmlp_ln_b', 'lam_q1', 'lam_k1', 'lam_q2', 'lam_k2',
        'diff_subln_g', 'w_out', 'ln1_g', 'ln1_b', 'w_gu', 'w_down', 'ln2_g', 'ln2_b', 'c_2', 'w_ada_2', 'b_ada_2',
        'g_mix_pre_2', 'g_mix_post_2', 'g_ff_pre_2', 'g_ff_post_2', 'w_in_2', 'b_f_2', 'w_pool_2', 'pool_scale_2',
        'conv_w_2', 'w_branch_2', 'w_out_2', 'w_ff1_2', 'w_ff2_2']


def kernel(**inputs):
    import numpy as np
    import concourse.bacc as bacc
    from concourse.bass_utils import run_bass_kernel_spmd

    nc = bacc.Bacc("TRN2", target_bir_lowering=False, num_devices=1)
    arrays, handles = {}, {}
    for name in _INS:
        a = np.ascontiguousarray(inputs[name])
        arrays[f"in_{name}"] = a
        handles[name] = nc.dram_tensor(f"in_{name}", a.shape, mybir.dt.from_np(a.dtype), kind="ExternalInput").ap()
    result = nc.dram_tensor("result", (1, S, D), F32, kind="ExternalOutput").ap()
    program(nc, handles, result)
    return run_bass_kernel_spmd(nc, [arrays], core_ids=[0]).results[0]["result"]
```
